# Optimizing a Trainium2 kernel written in Bass

```python
import jax, jax.numpy as jnp
from jax import lax
import numpy as np

D_MODEL = 1024
BATCH = 1
SEQ = 4096
DEPTH = 1

N_Q_HEADS = 8
N_KV_HEADS = 2
HEAD_DIM = D_MODEL // 16
ATTN_WIDTH = N_Q_HEADS * HEAD_DIM
KV_WIDTH = N_KV_HEADS * HEAD_DIM
WINDOW = 128
BLOCK = 128
POOL_WIDTH = D_MODEL // 2
POOL_WINDOWS = (2, 4, 8, 16)
N_POOL_GROUPS = 4
POOL_GROUP = POOL_WIDTH // N_POOL_GROUPS
IN_WIDTH = ATTN_WIDTH + 2 * KV_WIDTH + ATTN_WIDTH + 2 * POOL_WIDTH + 2 * D_MODEL
EPS = 1e-6
NEG_INF = -1e30

kernel_name = "hybrid_gated_swa_pool_encoder"

def rms_norm(x, g):
    xf = x.astype(jnp.float32)
    xf = xf * lax.rsqrt(jnp.mean(xf * xf, axis=-1, keepdims=True) + EPS)
    return (xf * g.astype(jnp.float32)).astype(x.dtype)

def windowed_gqa(q, k, v, sink):
    B, S, _ = q.shape
    nb = S // BLOCK
    G = N_Q_HEADS // N_KV_HEADS
    qb = q.reshape(B, nb, BLOCK, N_KV_HEADS, G, HEAD_DIM)
    pad = ((0, 0), (BLOCK, BLOCK), (0, 0))
    kp = jnp.pad(k, pad).reshape(B, nb + 2, BLOCK, N_KV_HEADS, HEAD_DIM)
    vp = jnp.pad(v, pad).reshape(B, nb + 2, BLOCK, N_KV_HEADS, HEAD_DIM)
    kw = jnp.concatenate([kp[:, :-2], kp[:, 1:-1], kp[:, 2:]], axis=2)
    vw = jnp.concatenate([vp[:, :-2], vp[:, 1:-1], vp[:, 2:]], axis=2)

    scale = HEAD_DIM ** -0.5
    scores = jnp.einsum('bnqhgd,bnkhd->bnhgqk', qb, kw,
                        preferred_element_type=jnp.float32) * scale

    r = jnp.arange(BLOCK)
    j = jnp.arange(3 * BLOCK)
    rel = r[:, None] - (j[None, :] - BLOCK)
    dist = jnp.abs(rel).astype(jnp.float32)
    kpos = jnp.arange(nb)[:, None] * BLOCK - BLOCK + j[None, :]
    valid = (kpos >= 0) & (kpos < S)
    mask = (jnp.abs(rel) <= WINDOW)[None] & valid[:, None, :]

    slopes = jnp.exp2(-8.0 * jnp.arange(1, N_Q_HEADS + 1, dtype=jnp.float32) / N_Q_HEADS)
    slopes = slopes.reshape(N_KV_HEADS, G)
    alibi = -slopes[:, :, None, None] * dist[None, None]
    scores = jnp.where(mask[None, :, None, None], scores + alibi[None, None], NEG_INF)

    sink_f = sink.astype(jnp.float32).reshape(N_KV_HEADS, G)[None, None, :, :, None]
    m = jnp.maximum(jnp.max(scores, axis=-1), sink_f)
    p = jnp.exp(scores - m[..., None])
    denom = jnp.sum(p, axis=-1) + jnp.exp(sink_f - m)
    out = jnp.einsum('bnhgqk,bnkhd->bnqhgd', p, vw.astype(jnp.float32))
    out = out / jnp.transpose(denom, (0, 1, 4, 2, 3))[..., None]
    return out.reshape(B, S, ATTN_WIDTH).astype(q.dtype)

def multiscale_pool(u, pool_w, pool_scale):
    B, S, _ = u.shape
    uf = u.astype(jnp.float32).reshape(B, S, N_POOL_GROUPS, POOL_GROUP)
    csum = jnp.pad(jnp.cumsum(uf, axis=1), ((0, 0), (1, 0), (0, 0), (0, 0)))
    t = jnp.arange(S)
    outs = []
    for gi, w in enumerate(POOL_WINDOWS):
        lo = jnp.clip(t - w // 2, 0, S)
        hi = jnp.clip(t + w // 2, 0, S)
        window_sum = csum[:, hi, gi] - csum[:, lo, gi]
        outs.append(window_sum / (hi - lo).astype(jnp.float32)[None, :, None])
    pooled = jnp.stack(outs, axis=2) - uf
    mixed = jnp.einsum('bsgc,gcd->bsgd', pooled.astype(u.dtype), pool_w)
    mixed = mixed * pool_scale.reshape(N_POOL_GROUPS, POOL_GROUP)
    return mixed.reshape(B, S, POOL_WIDTH)

def setup_inputs(seed: int = 0) -> dict:
    key = jax.random.key(seed)
    ks = jax.random.split(key, 11)
    f32 = jnp.float32
    x = jax.random.normal(ks[0], (BATCH, SEQ, D_MODEL), f32)
    norm_g = 1.0 + 0.1 * jax.random.normal(ks[1], (DEPTH, D_MODEL), f32)
    w_in = jax.random.normal(ks[2], (DEPTH, D_MODEL, IN_WIDTH), f32) * D_MODEL ** -0.5
    attn_sink = jax.random.normal(ks[3], (DEPTH, N_Q_HEADS), f32)
    pool_w = jax.random.normal(ks[4], (DEPTH, N_POOL_GROUPS, POOL_GROUP, POOL_GROUP), f32) * POOL_GROUP ** -0.5
    pool_scale = 1.0 + 0.1 * jax.random.normal(ks[5], (DEPTH, POOL_WIDTH), f32)
    w_branch_a = jax.random.normal(ks[6], (DEPTH, ATTN_WIDTH, D_MODEL), f32) * ATTN_WIDTH ** -0.5
    w_branch_b = jax.random.normal(ks[7], (DEPTH, POOL_WIDTH, D_MODEL), f32) * POOL_WIDTH ** -0.5
    w_out = jax.random.normal(ks[8], (DEPTH, D_MODEL, D_MODEL), f32) * D_MODEL ** -0.5
    final_norm_g = 1.0 + 0.1 * jax.random.normal(ks[9], (D_MODEL,), f32)
    return {"x": x, "norm_g": norm_g, "w_in": w_in, "attn_sink": attn_sink,
            "pool_w": pool_w, "pool_scale": pool_scale, "w_branch_a": w_branch_a,
            "w_branch_b": w_branch_b, "w_out": w_out, "final_norm_g": final_norm_g}

def reference(x, norm_g, w_in, attn_sink, pool_w, pool_scale, w_branch_a, w_branch_b, w_out, final_norm_g):
    widths = (ATTN_WIDTH, KV_WIDTH, KV_WIDTH, ATTN_WIDTH, POOL_WIDTH, POOL_WIDTH, D_MODEL)
    offsets = []
    acc = 0
    for wd in widths:
        acc += wd
        offsets.append(acc)
    for l in range(DEPTH):
        h = rms_norm(x, norm_g[l])
        proj = jnp.einsum('bsd,de->bse', h, w_in[l])
        q, k, v, z_a, u_b, z_b, g_a, g_b = jnp.split(proj, offsets, axis=-1)
        attn = windowed_gqa(q, k, v, attn_sink[l]) * jax.nn.silu(z_a)
        y_a = jnp.einsum('bsc,cd->bsd', attn, w_branch_a[l])
        pool = multiscale_pool(u_b, pool_w[l], pool_scale[l]) * jax.nn.silu(z_b)
        y_b = jnp.einsum('bsc,cd->bsd', pool, w_branch_b[l])
        merged = jax.nn.sigmoid(g_a) * y_a + jax.nn.sigmoid(g_b) * y_b
        x = x + jnp.einsum('bsd,de->bse', merged, w_out[l])
    return rms_norm(x, final_norm_g)


_drawn_inputs = setup_inputs


def setup_inputs(seed=0):
    import zlib

    import numpy as np

    out = dict(_drawn_inputs(seed))
    spreads = {}
    factors = {'attn_sink': 6.813}
    for name, (base, spread) in spreads.items():
        noise = np.random.default_rng([zlib.crc32(name.encode()), seed]).standard_normal(out[name].shape)
        drawn = base * np.exp(spread * noise) if base else spread * noise
        out[name] = __import__('jax').numpy.asarray(drawn.astype(out[name].dtype))
    for name, factor in factors.items():
        out[name] = (out[name] * factor).astype(out[name].dtype)
    return out
```

```python
from contextlib import ExitStack

import concourse.bass as bass
from concourse import mybir

F32 = mybir.dt.float32
F32R = mybir.dt.float32r
BF16 = mybir.dt.bfloat16
ALU = mybir.AluOpType
ACT = mybir.ActivationFunctionType

P = 128
D = 1024
S = 4096
HD = 64
NH = 8
G = 4
WINDOWS = (2, 4, 8, 16)
NG = len(WINDOWS)
EPS = 1e-6
MASKED = -1e30
T = 512
NB = T // P
CHUNKS = S // T
LAST = CHUNKS - 1
KD = D // P
HW = T + P
KW = T + 2 * P
LEFT = 8
UW = LEFT + HW
FRESH = LEFT + P
UNITS = 2 * NB

HEAD_TILES = [("k", 0), ("v", 0)] + [("q", j) for j in range(4)] + [("za", j) for j in range(4)]
STEPS = [[("u", 0)], [("zb", 0)], [("u", 1), ("mix", 0)], [("zb", 1)], [("u", 2), ("mix", 1)],
         [("zb", 2)], [("u", 3), ("mix", 2)], [("zb", 3)], [("ga", 0), ("mix", 3)]]
GATE_TILES = [(k, j) for j in range(KD) for k in ("ga", "gb", "ab")][1:]
OUT_TILES = [("out", i) for i in range(8)]
TILES = HEAD_TILES + [t for s in STEPS for t in s] + GATE_TILES + OUT_TILES
NW = len(TILES)
SPLITS = 3
RAWS = 2
INDEX = {t: w for w, t in enumerate(TILES)}
DENSE = [t for t in TILES if t[0] not in ("ab", "out")]
DVE_LAST = [t for t in DENSE if t[0] in ("k", "q", "za", "zb", "mix")]
ACT_LAST = [t for t in DENSE if t[0] in ("v", "u", "ga", "gb")]
assert NW % SPLITS == 0 and NW % RAWS == 0 and len(DENSE) % 2 == 0


def cols_of(kind):
    return P if kind == "mix" else D


def build(nc, x, w_in_t, w_ab_t, w_out_t, pool_w, attn_sink, pool_scale, norm_g, final_g, out):
    with ExitStack() as ctx:
        def sb(name, shape, dt=F32):
            return ctx.enter_context(nc.sbuf_tensor(name, shape, dt))

        def sem(name):
            return ctx.enter_context(nc.semaphore(name))

        h_hi = sb("h_hi", [P, KD, HW], F32R)
        h_lo = sb("h_lo", [P, KD, HW], F32R)
        qa_hi = sb("qa_hi", [P, 4, T], F32R)
        qa_lo = sb("qa_lo", [P, 4, T], F32R)
        po_hi = sb("po_hi", [P, NG, T], F32R)
        po_lo = sb("po_lo", [P, NG, T], F32R)
        arena_r = sb("arena_r", [P, 8 * 2 * T], F32R)
        arena_f = sb("arena_f", [P, 6 * D])
        k_hi = sb("k_hi", [P, KW], F32R)
        k_lo = sb("k_lo", [P, KW], F32R)
        v_hi = sb("v_hi", [P, KW // P, P], F32R)
        v_lo = sb("v_lo", [P, KW // P, P], F32R)
        u = sb("u", [P, NG, UW])
        sums = sb("sums", [P, 2, T + 16])
        raw = sb("raw", [P, RAWS, D])
        w_hi = sb("w_hi", [P, SPLITS, D], F32R)
        w_lo = sb("w_lo", [P, SPLITS, D], F32R)
        bias = sb("bias", [P, NH, 3 * P], BF16)
        g_norm = sb("g_norm", [P, D])
        g_final = sb("g_final", [P, D])
        ident = sb("ident", [P, P])
        eps = sb("eps", [P, 1])
        minus_half = sb("minus_half", [P, 1])
        recip = sb("recip", [P, 16])
        recip_down = sb("recip_down", [P, 16])
        sink = sb("sink", [P, NH])
        minus_sink = sb("minus_sink", [P, NH])
        half_scale = sb("half_scale", [P, NG])
        row_max = sb("row_max", [P, 2, G])
        minus_max = sb("minus_max", [P, 2, G])
        row_sum = sb("row_sum", [P, 2, G])
        sink_term = sb("sink_term", [P, 2, G])
        waiter = sb("waiter", [P, 2, G])
        ssq = sb("ssq", [P, 8])
        ms = sb("ms", [P, 8])
        rstd = sb("rstd", [P, 8])

        v_t = arena_f[:, 0:HW]
        p = arena_f[:, 0:2 * G * 3 * P].rearrange("p (b h k) -> p b h k", b=2, h=G)
        za = arena_f[:, 3 * D:5 * D].rearrange("p (j t) -> p j t", j=4)
        zb = arena_f[:, 5 * D:6 * D].rearrange("p (j t) -> p j t", j=2)
        gate = arena_f[:, 0:2 * D].rearrange("p (b a t) -> p b a t", b=2, a=2)
        xn = arena_f[:, 0:2 * D].rearrange("p (b f) -> p b f", b=2)
        y = arena_f[:, 2 * D:6 * D].rearrange("p (m f) -> p m f", m=NB)
        prod = sb("prod", [P, G, P])
        junk = sums[:, :, :].rearrange("p a b -> p (a b)").bitcast(BF16)[:, 0:D]
        pt_hi = [arena_r[:, kt * 2 * T:kt * 2 * T + T] for kt in range(3)]
        pt_lo = [arena_r[:, kt * 2 * T + T:(kt + 1) * 2 * T] for kt in range(3)]
        pooled_hi = arena_r[:, 6 * T:7 * T]
        pooled_lo = arena_r[:, 7 * T:8 * T]
        mg_hi = [arena_r[:, j * 2 * T:j * 2 * T + T] for j in range(KD)]
        mg_lo = [arena_r[:, j * 2 * T + T:(j + 1) * 2 * T] for j in range(KD)]

        bank = [ctx.enter_context(nc.psum_tensor(f"bank{i}", [P, T], F32)) for i in range(8)]
        pv_bank, t_bank = bank[2], bank[3:6]

        s_const = sem("s_const")
        s_made = sem("s_made")
        s_abs = sem("s_abs")
        s_cdve = sem("s_cdve")
        raw_in = [sem(f"raw_in{i}") for i in range(RAWS)]
        split_hi = sem("split_hi")
        split_lo = sem("split_lo")
        tile_done = sem("tile_done")
        act_read = sem("act_read")
        dve_read = sem("dve_read")
        hi_kq = sem("hi_kq")
        tanh_z = sem("tanh_z")
        v_turned = sem("v_turned")
        v_hi_done = sem("v_hi_done")
        v_lo_done = sem("v_lo_done")
        qk_done = sem("qk_done")
        max_done = sem("max_done")
        neg_done = sem("neg_done")
        sink_in = sem("sink_in")
        exp_done = sem("exp_done")
        den_done = sem("den_done")
        norm_done = sem("norm_done")
        pt_done = sem("pt_done")
        pt_hi_done = sem("pt_hi_done")
        pt_lo_done = sem("pt_lo_done")
        pv_done = sem("pv_done")
        prod_done = sem("prod_done")
        at_hi_done = sem("at_hi_done")
        at_lo_done = sem("at_lo_done")
        sum_step = sem("sum_step")
        pooled_f = sem("pooled_f")
        edge_done = sem("edge_done")
        pooled_h = sem("pooled_h")
        pooled_l = sem("pooled_l")
        po_hi_done = sem("po_hi_done")
        po_lo_done = sem("po_lo_done")
        gated = sem("gated")
        merged_f = sem("merged_f")
        merged_h = sem("merged_h")
        merged_l = sem("merged_l")
        kvu_moved = sem("kvu_moved")
        h_moved = sem("h_moved")
        x_in = [sem(f"x_in{i}") for i in range(2)]
        x_sq = sem("x_sq")
        x_ms = sem("x_ms")
        x_rstd = sem("x_rstd")
        x_norm = sem("x_norm")
        x_turned = sem("x_turned")
        h_hi_done = sem("h_hi_done")
        h_lo_done = sem("h_lo_done")
        res_in = [sem(f"res_in{m}") for m in range(NB)]
        out_done = sem("out_done")
        y_done = sem("y_done")
        y_sq = sem("y_sq")
        y_ms = sem("y_ms")
        y_rstd = sem("y_rstd")
        y_norm = sem("y_norm")
        stored = [sem(f"stored{m}") for m in range(NB)]

        N_CONST = 4
        AHEAD = NB + 1

        def count(c, per, i, unit=1):
            value = (c * per + i) * unit
            return max(value, 0) if isinstance(c, int) else value

        def last_read(c, t, back=0):
            if t in DVE_LAST:
                return dve_read, count(c, len(DVE_LAST), DVE_LAST.index(t) + 1 - back * len(DVE_LAST))
            return act_read, count(c, len(ACT_LAST), ACT_LAST.index(t) + 1 - back * len(ACT_LAST))

        def dense_bank(t):
            return bank[6 + DENSE.index(t) % 2]

        def fresh(c):
            return T - P if is_last(c) else T

        def is_first(c):
            return isinstance(c, int) and c == 0

        def is_last(c):
            return isinstance(c, int) and c == LAST

        def key_tiles(c, b):
            lo = 1 if is_first(c) and b == 0 else 0
            hi = 2 if is_last(c) and b == NB - 1 else 3
            return lo, hi

        def over_chunks(eng, chunk):
            chunk(0)
            with eng.Fori(1, LAST) as c:
                chunk(c)
            chunk(LAST)

        def signals(lo, hi, kt):
            return 2 if (lo == 1 and kt == 1) or (hi == 2 and kt == 1) else 1

        def pooled_at(g):
            return sums[:, 1 - g % 2, 0:T]

        block = ctx.enter_context(nc.Block())

        @block.sync
        def _(sp):
            def load_weight(c, w):
                kind, j = TILES[w]
                n = cols_of(kind)
                at = {"q": 0, "k": 4, "v": 5, "za": 6, "u": 10, "zb": 14, "ga": 18, "gb": 26}
                src = (pool_w[j] if kind == "mix" else w_ab_t[j] if kind == "ab" else
                       w_out_t[j] if kind == "out" else w_in_t[at[kind] + j])
                sp.wait_ge(split_lo, count(c, NW, w + 1 - RAWS))
                sp.dma_start(raw[:, w % RAWS, 0:n], src).then_inc(raw_in[w % RAWS], 16)

            def load_rows(c, m):
                if m < 2:
                    sp.wait_ge(merged_l, count(c, KD, KD))
                else:
                    sp.wait_ge(x_turned, count(c, NB, AHEAD + m - 1))
                slot = (AHEAD + m) % 2
                tile = (c * NB + AHEAD + m) % (S // P)
                sp.dma_start(xn[:, slot, :], x[bass.ds(tile * P, P), :]).then_inc(x_in[slot], 16)

            def chunk(c):
                for w in range(NW):
                    if w == INDEX[("ga", 2)]:
                        sp.wait_ge(pt_done, count(c, 3 * UNITS, 3 * UNITS))
                        sp.wait_ge(prod_done, count(c, UNITS, UNITS))
                        sp.wait_ge(po_lo_done, count(c, NG, NG))
                        for m in range(NB):
                            sp.dma_start(y[:, m, :], x[bass.ds(c * T + m * P, P), :])\
                              .then_inc(res_in[m], 16)
                    if not is_last(c):
                        if w == INDEX[("out", 4)]:
                            load_rows(c, 0)
                            load_rows(c, 1)
                        if w == INDEX[("out", 7)]:
                            load_rows(c, 2)
                    if not (is_first(c) and w < RAWS):
                        load_weight(c, w)
                if not is_last(c):
                    load_rows(c, 3)

            sp.dma_start(xn[:, 0, :], x[0:P, :]).then_inc(x_in[0], 16)
            sp.dma_start(xn[:, 1, :], x[P:2 * P, :]).then_inc(x_in[1], 16)
            for w in range(RAWS):
                load_weight(0, w)
            for i in range(2, AHEAD):
                sp.wait_ge(x_turned, i - 1)
                sp.dma_start(xn[:, i % 2, :], x[i * P:(i + 1) * P, :]).then_inc(x_in[i % 2], 16)
            over_chunks(sp, chunk)
            for m in range(NB):
                sp.wait_ge(stored[m], 16 * CHUNKS)

        @block.gpsimd
        def _(pool):
            nc.gpsimd.memset(ident[:, :], 0.0).then_inc(s_made, 1)
            nc.gpsimd.memset(eps[:, :], EPS).then_inc(s_made, 1)
            nc.gpsimd.memset(minus_half[:, :], -0.5).then_inc(s_made, 1)
            nc.gpsimd.memset(u[:, :, 0:LEFT], 0.0).then_inc(s_made, 1)
            pool.wait_ge(s_made, 4)
            nc.gpsimd.affine_select(out=ident[:, :], in_=ident[:, :], compare_op=ALU.not_equal, fill=1.0,
                                    base=0, pattern=[[-1, P]], channel_multiplier=1).then_inc(s_made, 1)

            def rstd_of(c, per, i, col, sq, ms_sem, rs_sem):
                pool.wait_ge(sq, count(c, per, i))
                nc.gpsimd.tensor_tensor(ms[:, col:col + 1], ssq[:, col:col + 1], eps[:, :],
                                        ALU.add).then_inc(ms_sem, 1)
                pool.wait_ge(ms_sem, count(c, per, i))
                nc.gpsimd.tensor_tensor(rstd[:, col:col + 1], ms[:, col:col + 1], minus_half[:, :],
                                        ALU.pow).then_inc(rs_sem, 1)

            for i in range(2):
                rstd_of(0, 0, i + 1, 4 + i % 2, x_sq, x_ms, x_rstd)
            dist = arena_f[:, 3 * D:3 * D + 3 * P]
            nc.gpsimd.iota(dist, pattern=[[-1, 3 * P]], base=P, channel_multiplier=1,
                           allow_small_or_imprecise_dtypes=True).then_inc(s_made, 1)
            nc.gpsimd.iota(recip[:, :], pattern=[[1, 16]], base=1, channel_multiplier=0,
                           allow_small_or_imprecise_dtypes=True).then_inc(s_made, 1)
            nc.gpsimd.iota(recip_down[:, :], pattern=[[-1, 16]], base=16, channel_multiplier=0,
                           allow_small_or_imprecise_dtypes=True).then_inc(s_made, 1)
            for i in range(2, AHEAD):
                rstd_of(0, 0, i + 1, 4 + i % 2, x_sq, x_ms, x_rstd)
            pool.wait_ge(s_cdve, 8)
            nc.gpsimd.affine_select(out=bias[:, :, :], in_=bias[:, :, :], compare_op=ALU.is_ge, fill=MASKED,
                                    base=0, pattern=[[0, NH], [1, 3 * P]], channel_multiplier=-1)\
                     .then_inc(s_made, 1)
            pool.wait_ge(s_made, 9)
            nc.gpsimd.affine_select(out=bias[:, :, :], in_=bias[:, :, :], compare_op=ALU.is_ge, fill=MASKED,
                                    base=2 * P, pattern=[[0, NH], [-1, 3 * P]], channel_multiplier=1)\
                     .then_inc(s_made, 1)

            def chunk(c):
                if is_last(c):
                    pool.wait_ge(kvu_moved, 5 * LAST)
                    end = LEFT + T
                    nc.gpsimd.memset(u[:, :, end:end + LEFT], 0.0).then_inc(s_made, 1)
                    pool.wait_ge(s_made, 11)
                done = 0
                for g, win in enumerate(WINDOWS):
                    a = LEFT - win // 2
                    step, width, src = 1, T + win - 2, u[:, g, a:a + T + win - 1]
                    pool.wait_ge(*last_read(c, ("u", g)))
                    if g:
                        pool.wait_ge(pooled_l, count(c, NG, g))
                    else:
                        pool.wait_ge(y_sq, count(c, NB, 0))
                        pool.wait_ge(pooled_l, count(c, NG, 0))
                    which = 0
                    while True:
                        dst = sums[:, which, 0:width]
                        if step > 1:
                            pool.wait_ge(sum_step, count(c, 10, done))
                        nc.gpsimd.tensor_tensor(dst, src[:, 0:width], src[:, step:step + width],
                                                ALU.add).then_inc(sum_step, 1)
                        done += 1
                        step *= 2
                        if step == win:
                            break
                        src, which, width = sums[:, which, :], 1 - which, width - step
                if not is_last(c):
                    for m in range(NB):
                        rstd_of(c, NB, AHEAD + m + 1, 4 + (AHEAD + m) % 2, x_sq, x_ms, x_rstd)
                for m in range(NB):
                    rstd_of(c, NB, m + 1, m, y_sq, y_ms, y_rstd)

            over_chunks(pool, chunk)

        @block.scalar
        def _(act):
            def split(c, w):
                if w >= NW and is_last(c):
                    return
                n = cols_of(TILES[w % NW][0])
                act.wait_ge(raw_in[w % RAWS], count(c, NW // RAWS, w // RAWS + 1, 16))
                act.wait_ge(tile_done, count(c, NW, w - SPLITS + 1))
                nc.scalar.activation(w_hi[:, w % SPLITS, 0:n], raw[:, w % RAWS, 0:n],
                                     ACT.Copy).then_inc(split_hi, 1)

            def rows_square(c, per, i, slot, load):
                act.wait_ge(x_in[slot], count(c, per // 2, load, 16))
                act.wait_ge(x_ms, count(c, per, i - 2))
                act.wait_ge(x_sq, count(c, per, i - 1))
                nc.scalar.activation(junk, xn[:, slot, :], ACT.Square, scale=D ** -0.5,
                                     accum_out=ssq[:, 4 + slot:5 + slot]).then_inc(x_sq, 1)

            def rows_hi(c, per, i, at):
                act.wait_ge(x_turned, count(c, per, i))
                for half in range(2):
                    ins = nc.scalar.activation(
                        h_hi[:, 4 * half:4 * half + 4, at:at + P],
                        bank[4 + half][:, :].rearrange("p (k t) -> p k t", k=4), ACT.Copy)
                ins.then_inc(h_hi_done, 1)

            act.dma_start(g_norm[:, :], norm_g.to_broadcast([P, D])).then_inc(s_const, 16)
            act.dma_start(sink[:, :], attn_sink.to_broadcast([P, NH])).then_inc(s_const, 16)
            with nc.allow_non_contiguous_dma("512 values, once"):
                act.dma_start(half_scale[:, :], pool_scale.rearrange("g p -> p g")).then_inc(s_const, 16)
            act.dma_start(g_final[:, :], final_g.to_broadcast([P, D])).then_inc(s_const, 16)
            for i in range(AHEAD):
                rows_square(0, 0, i + 1, i % 2, i // 2 + 1)
                if i:
                    rows_hi(0, 0, i, (i - 1) * P)
                if i == 2:
                    act.wait_ge(s_made, 6)
                    dist = arena_f[:, 3 * D:3 * D + 3 * P]
                    nc.scalar.activation(dist, dist, ACT.Abs).then_inc(s_abs, 1)
                if 1 <= i <= RAWS:
                    split(0, i - 1)
            rows_hi(0, 0, AHEAD, (AHEAD - 1) * P)
            split(0, RAWS)

            def evacuate(c, t):
                kind, j = t
                src = dense_bank(t)
                act.wait_ge(tile_done, count(c, NW, INDEX[t] + 1))
                n = fresh(c)
                if kind == "k":
                    act.wait_ge(kvu_moved, count(c, 5, 0))
                    ins = nc.scalar.activation(k_hi[:, 2 * P:2 * P + n], src[:, 0:n], ACT.Copy)
                    if is_first(c):
                        ins = nc.scalar.activation(k_hi[:, P:2 * P], bank[0][:, 0:P], ACT.Copy)
                    ins.then_inc(hi_kq, 1)
                elif kind == "v":
                    ins = nc.scalar.activation(v_t[:, 0:n], src[:, 0:n], ACT.Copy)
                    if is_first(c):
                        ins = nc.scalar.activation(v_t[:, T:T + P], bank[1][:, 0:P], ACT.Copy)
                    ins.then_inc(act_read, 1)
                elif kind == "q":
                    act.wait_ge(tile_done, count(c, NW, INDEX[("ab", KD - 1)] + 1 - NW))
                    nc.scalar.activation(qa_hi[:, j, :], src[:, :], ACT.Copy,
                                         scale=HD ** -0.5).then_inc(hi_kq, 1)
                elif kind == "za":
                    if j == 0:
                        for m in range(NB):
                            act.wait_ge(stored[m], count(c, 1, 0, 16))
                    nc.scalar.activation(za[:, j, :], src[:, :], ACT.Tanh, scale=0.5).then_inc(tanh_z, 1)
                elif kind == "zb":
                    if j >= 2:
                        act.wait_ge(po_lo_done, count(c, NG, j - 1))
                    nc.scalar.activation(zb[:, j % 2, :], src[:, :], ACT.Tanh, scale=0.5)\
                      .then_inc(tanh_z, 1)
                elif kind == "u":
                    act.wait_ge(kvu_moved, count(c, 5, 0))
                    ins = nc.scalar.activation(u[:, j, FRESH:FRESH + n], src[:, 0:n], ACT.Copy)
                    if is_first(c):
                        ins = nc.scalar.activation(u[:, j, LEFT:FRESH], pv_bank[:, 0:P], ACT.Copy)
                    ins.then_inc(act_read, 1)
                elif kind in ("ga", "gb"):
                    if j < 2:
                        act.wait_ge(pt_done, count(c, 3 * UNITS, 3 * UNITS))
                    else:
                        act.wait_ge(merged_l, count(c, KD, j - 1))
                    nc.scalar.activation(gate[:, j % 2, "ab".index(kind[1]), :], src[:, :], ACT.Tanh,
                                         scale=0.5).then_inc(act_read, 1)

            def exps(c, n):
                b, kv = divmod(n, 2)
                lo, hi = key_tiles(c, b)
                act.wait_ge(neg_done, count(c, UNITS, n + 1))
                for j in range(G):
                    pj = p[:, n % 2, j, lo * P:hi * P]
                    nc.scalar.activation(pj, pj, ACT.Exp, bias=minus_max[:, n % 2, j:j + 1],
                                         accum_out=row_sum[:, n % 2, j:j + 1])
                act.wait_ge(sink_in, count(c, UNITS, n + 1))
                nc.scalar.activation(sink_term[:, n % 2, :], sink_term[:, n % 2, :],
                                     ACT.Exp).then_inc(exp_done, 1)

            def pt_his(c, n):
                lo, hi = key_tiles(c, n // 2)
                for kt in range(lo, hi):
                    act.wait_ge(pt_done, count(c, 3 * UNITS, 3 * n + kt + 1))
                    act.wait_ge(pv_done, count(c, UNITS, n))
                    nc.scalar.activation(pt_hi[kt], t_bank[kt][:, :], ACT.Copy)\
                      .then_inc(pt_hi_done, signals(lo, hi, kt))

            def attention_hi(c, b):
                act.wait_ge(prod_done, count(c, UNITS, 2 * b + 2))
                nc.scalar.activation(qa_hi[:, :, b * P:(b + 1) * P], prod[:, :, :],
                                     ACT.Copy).then_inc(at_hi_done, 1)

            def pooled_his(c, g):
                act.wait_ge(pooled_f, count(c, NG, g + 1))
                act.wait_ge(tile_done, count(c, NW, INDEX[("mix", g - 1)] + 1 if g else 0))
                nc.scalar.activation(pooled_hi, pooled_at(g), ACT.Copy).then_inc(pooled_h, 1)

            def pool_out_hi(c, g):
                act.wait_ge(dve_read, count(c, len(DVE_LAST), DVE_LAST.index(("mix", g)) + 1))
                nc.scalar.activation(po_hi[:, g, :], zb[:, g % 2, :], ACT.Copy).then_inc(po_hi_done, 1)

            def chunk(c):
                w = 0
                for t in HEAD_TILES:
                    evacuate(c, t)
                    split(c, w + SPLITS)
                    w += 1
                    if t == ("q", 1):
                        act.wait_ge(v_turned, count(c, 1, 1))
                        nt = fresh(c) // P
                        act.wait_ge(kvu_moved, count(c, 5, 0))
                        ins = nc.scalar.activation(
                            v_hi[:, 2:2 + nt, :],
                            t_bank[0][:, 0:nt * P].rearrange("p (b f) -> p b f", f=P), ACT.Copy)
                        if is_first(c):
                            ins = nc.scalar.activation(v_hi[:, 1, :], t_bank[1][:, 0:P], ACT.Copy)
                        ins.then_inc(v_hi_done, 1)
                for s, tiles in enumerate(STEPS):
                    if s >= 3 and s % 2 == 1:
                        attention_hi(c, (s - 3) // 2)
                    if s < UNITS:
                        exps(c, s)
                    if s >= 2 and s % 2 == 0:
                        pooled_his(c, s // 2 - 1)
                    if s:
                        pt_his(c, s - 1)
                    for t in tiles:
                        evacuate(c, t) if t[0] != "mix" else pool_out_hi(c, t[1])
                        split(c, w + SPLITS)
                        w += 1
                attention_hi(c, NB - 1)
                for t in GATE_TILES:
                    if t[0] == "ab":
                        act.wait_ge(merged_f, count(c, KD, t[1] + 1))
                        nc.scalar.activation(mg_hi[t[1]], gate[:, t[1] % 2, 0, :],
                                             ACT.Copy).then_inc(merged_h, 1)
                    else:
                        evacuate(c, t)
                    split(c, w + SPLITS)
                    w += 1
                for i in range(8):
                    split(c, w + SPLITS)
                    w += 1
                    if not is_last(c):
                        if 2 <= i < 6:
                            if i == 2:
                                act.wait_ge(h_moved, count(c, 2, 2))
                            rows_hi(c, NB, AHEAD + i - 1, P + (i - 2) * P)
                        if i in (0, 1, 3, 4):
                            m = (0, 1, None, 2, 3)[i]
                            rows_square(c, NB, AHEAD + m + 1, (AHEAD + m) % 2, (AHEAD + m) // 2 + 1)
                for m in range(NB):
                    act.wait_ge(y_done, count(c, 8, NB + m + 1))
                    act.wait_ge(y_sq, count(c, NB, m))
                    nc.scalar.activation(junk, y[:, m, :], ACT.Square, scale=D ** -0.5,
                                         accum_out=ssq[:, m:m + 1]).then_inc(y_sq, 1)
                for m in range(NB):
                    act.wait_ge(y_norm, count(c, NB, m + 1))
                    act.dma_start(out[bass.ds(c * T + m * P, P), :], y[:, m, :]).then_inc(stored[m], 16)

            over_chunks(act, chunk)

        @block.vector
        def _(dve):
            def split(c, w):
                if w >= NW and is_last(c):
                    return
                n = cols_of(TILES[w % NW][0])
                dve.wait_ge(split_hi, count(c, NW, w + 1))
                nc.vector.tensor_tensor(w_lo[:, w % SPLITS, 0:n], raw[:, w % RAWS, 0:n],
                                        w_hi[:, w % SPLITS, 0:n].bitcast(F32),
                                        ALU.subtract).then_inc(split_lo, 1)

            def rows_norm(c, per, i, slot):
                dve.wait_ge(x_rstd, count(c, per, i))
                nc.vector.scalar_tensor_tensor(xn[:, slot, :], xn[:, slot, :], rstd[:, 4 + slot:5 + slot],
                                               g_norm[:, :], ALU.mult, ALU.mult).then_inc(x_norm, 1)

            def rows_lo(c, per, i, at):
                dve.wait_ge(h_hi_done, count(c, per, i))
                for half in range(2):
                    ks = slice(4 * half, 4 * half + 4)
                    ins = nc.vector.tensor_tensor(
                        h_lo[:, ks, at:at + P], bank[4 + half][:, :].rearrange("p (k t) -> p k t", k=4),
                        h_hi[:, ks, at:at + P].bitcast(F32), ALU.subtract)
                ins.then_inc(h_lo_done, 1)

            dve.wait_ge(s_const, 16 * N_CONST)
            for i in range(AHEAD):
                rows_norm(0, 0, i + 1, i % 2)
                if i:
                    rows_lo(0, 0, i, (i - 1) * P)
                if i == 2:
                    dve.wait_ge(s_abs, 1)
                    dist = arena_f[:, 3 * D:3 * D + 3 * P]
                    for hd in range(NH):
                        nc.vector.tensor_scalar(bias[:, hd, :], dist, -(2.0 ** -(hd + 1)), None,
                                                ALU.mult).then_inc(s_cdve, 1)
                if 1 <= i <= RAWS:
                    split(0, i - 1)
            rows_lo(0, 0, AHEAD, (AHEAD - 1) * P)
            split(0, RAWS)
            nc.vector.tensor_scalar(minus_sink[:, :], sink[:, :], -1.0, None, ALU.mult).then_inc(s_cdve, 1)
            nc.vector.tensor_scalar(half_scale[:, :], half_scale[:, :], 0.5, None,
                                    ALU.mult).then_inc(s_cdve, 1)
            dve.wait_ge(s_made, 8)
            nc.vector.reciprocal(recip[:, :], recip[:, :]).then_inc(s_cdve, 1)
            nc.vector.reciprocal(recip_down[:, :], recip_down[:, :]).then_inc(s_cdve, 1)
            dve.wait_ge(s_cdve, 8 + 4)
            dve.wait_ge(s_made, 10)

            def evacuate(c, t):
                kind, j = t
                src = dense_bank(t)
                n = fresh(c)
                if kind == "k":
                    dve.wait_ge(hi_kq, count(c, 5, 1))
                    ins = nc.vector.tensor_tensor(k_lo[:, 2 * P:2 * P + n], src[:, 0:n],
                                                  k_hi[:, 2 * P:2 * P + n].bitcast(F32), ALU.subtract)
                    if is_first(c):
                        ins = nc.vector.tensor_tensor(k_lo[:, P:2 * P], bank[0][:, 0:P],
                                                      k_hi[:, P:2 * P].bitcast(F32), ALU.subtract)
                    ins.then_inc(dve_read, 1)
                elif kind == "q":
                    dve.wait_ge(hi_kq, count(c, 5, j + 2))
                    nc.vector.scalar_tensor_tensor(qa_lo[:, j, :], src[:, :], HD ** -0.5,
                                                   qa_hi[:, j, :].bitcast(F32), ALU.mult,
                                                   ALU.subtract).then_inc(dve_read, 1)
                elif kind in ("za", "zb"):
                    dst = za[:, j, :] if kind == "za" else zb[:, j % 2, :]
                    dve.wait_ge(tanh_z, count(c, 8, (0 if kind == "za" else 4) + j + 1))
                    nc.vector.scalar_tensor_tensor(dst, dst, 1.0, src[:, :], ALU.add,
                                                   ALU.mult).then_inc(dve_read, 1)

            def maxima(c, n):
                b, kv = divmod(n, 2)
                lo, hi = key_tiles(c, b)
                for j in range(G):
                    dve.wait_ge(qk_done, count(c, 4 * UNITS, 4 * n + j + 1))
                    if j == 0:
                        dve.wait_ge(pt_done, count(c, 3 * UNITS, 3 * (n - 1)))
                    nc.vector.memset(waiter[:, n % 2, j:j + 1], 0.0)
                    nc.vector.tensor_tensor_reduce(
                        p[:, n % 2, j, lo * P:hi * P], bank[j % 2][:, lo * P:hi * P],
                        bias[:, kv * G + j, lo * P:hi * P], 1.0, -3.0e38, ALU.add, ALU.max,
                        row_max[:, n % 2, j:j + 1]).then_inc(max_done, 1)
                dve.wait_ge(max_done, count(c, 4 * UNITS, 4 * n + 4))
                nc.vector.scalar_tensor_tensor(minus_max[:, n % 2, :], row_max[:, n % 2, :], -1.0,
                                               minus_sink[:, kv * G:kv * G + G], ALU.mult,
                                               ALU.min).then_inc(neg_done, 1)
                dve.wait_ge(neg_done, count(c, UNITS, n + 1))
                nc.vector.tensor_tensor(sink_term[:, n % 2, :], sink[:, kv * G:kv * G + G],
                                        minus_max[:, n % 2, :], ALU.add).then_inc(sink_in, 1)

            def normalise(c, n):
                lo, hi = key_tiles(c, n // 2)
                dve.wait_ge(exp_done, count(c, UNITS, n + 1))
                nc.vector.tensor_tensor(row_sum[:, n % 2, :], row_sum[:, n % 2, :],
                                        sink_term[:, n % 2, :], ALU.add).then_inc(den_done, 1)
                dve.wait_ge(den_done, count(c, 2 * UNITS, 2 * n + 1))
                nc.vector.reciprocal(row_sum[:, n % 2, :], row_sum[:, n % 2, :]).then_inc(den_done, 1)
                dve.wait_ge(den_done, count(c, 2 * UNITS, 2 * n + 2))
                for j in range(G):
                    pj = p[:, n % 2, j, lo * P:hi * P]
                    ins = nc.vector.tensor_scalar(pj, pj, row_sum[:, n % 2, j:j + 1], 0.5, ALU.mult,
                                                  ALU.mult)
                ins.then_inc(norm_done, 1)

            def pt_los(c, n):
                lo, hi = key_tiles(c, n // 2)
                for kt in range(lo, hi):
                    dve.wait_ge(pt_hi_done, count(c, 3 * UNITS, 3 * n + kt + 1))
                    nc.vector.tensor_tensor(pt_lo[kt], t_bank[kt][:, :], pt_hi[kt].bitcast(F32),
                                            ALU.subtract).then_inc(pt_lo_done, signals(lo, hi, kt))

            def product(c, n):
                b, kv = divmod(n, 2)
                rows = slice(kv * HD, (kv + 1) * HD)
                dve.wait_ge(pv_done, count(c, UNITS, n + 1))
                dve.wait_ge(at_lo_done, count(c, NB, b))
                nc.vector.tensor_tensor(prod[rows, :, :],
                                        pv_bank[rows, :].rearrange("p (j q) -> p j q", j=G),
                                        za[rows, :, b * P:(b + 1) * P], ALU.mult).then_inc(prod_done, 1)

            def attention_lo(c, b):
                dve.wait_ge(at_hi_done, count(c, NB, b + 1))
                nc.vector.tensor_tensor(qa_lo[:, :, b * P:(b + 1) * P], prod[:, :, :],
                                        qa_hi[:, :, b * P:(b + 1) * P].bitcast(F32),
                                        ALU.subtract).then_inc(at_lo_done, 1)

            def pooled(c, g):
                win = WINDOWS[g]
                total = sums[:, g % 2, :]
                here = u[:, g, LEFT:LEFT + T]
                dve.wait_ge(sum_step, count(c, 10, (g + 1) * (g + 2) // 2))
                lo = win // 2 if is_first(c) else 0
                hi = T - (win // 2 - 1) if is_last(c) else T
                ends = []
                if lo:
                    ends.append((slice(0, lo), recip[:, win // 2 - 1:win - 1]))
                if hi < T:
                    ends.append((slice(hi, T), recip_down[:, 16 - win + 1:16 - win // 2]))
                for cols, r in ends:
                    nc.vector.tensor_tensor(total[:, cols], total[:, cols], r, ALU.mult)\
                      .then_inc(edge_done, 1)
                    edges[0] += 1
                    dve.wait_ge(edge_done, edges[0])
                    nc.vector.tensor_tensor(pooled_at(g)[:, cols], total[:, cols], here[:, cols],
                                            ALU.subtract)
                nc.vector.scalar_tensor_tensor(pooled_at(g)[:, lo:hi], total[:, lo:hi], 1.0 / win,
                                               here[:, lo:hi], ALU.mult, ALU.subtract)\
                  .then_inc(pooled_f, 1)

            edges = [0]

            def pooled_los(c, g):
                dve.wait_ge(pooled_h, count(c, NG, g + 1))
                nc.vector.tensor_tensor(pooled_lo, pooled_at(g), pooled_hi.bitcast(F32),
                                        ALU.subtract).then_inc(pooled_l, 1)

            def pool_out(c, g):
                dve.wait_ge(tile_done, count(c, NW, INDEX[("mix", g)] + 1))
                nc.vector.scalar_tensor_tensor(zb[:, g % 2, :], dense_bank(("mix", g))[:, :],
                                               half_scale[:, g:g + 1], zb[:, g % 2, :], ALU.mult,
                                               ALU.mult).then_inc(dve_read, 1)
                dve.wait_ge(po_hi_done, count(c, NG, g + 1))
                nc.vector.tensor_tensor(po_lo[:, g, :], zb[:, g % 2, :], po_hi[:, g, :].bitcast(F32),
                                        ALU.subtract).then_inc(po_lo_done, 1)

            def merge(c, j):
                dve.wait_ge(tile_done, count(c, NW, INDEX[("ab", j)] + 1))
                dve.wait_ge(*last_read(c, ("gb", j)))
                for a in range(2):
                    gt = gate[:, j % 2, a, :]
                    nc.vector.scalar_tensor_tensor(gt, gt, 1.0, bank[2 * (j % 2) + a][:, :], ALU.add,
                                                   ALU.mult).then_inc(gated, 1)
                dve.wait_ge(gated, count(c, 2 * KD, 2 * j + 2))
                nc.vector.tensor_tensor(gate[:, j % 2, 0, :], gate[:, j % 2, 0, :], gate[:, j % 2, 1, :],
                                        ALU.add).then_inc(merged_f, 1)
                dve.wait_ge(merged_h, count(c, KD, j + 1))
                nc.vector.tensor_tensor(mg_lo[j], gate[:, j % 2, 0, :], mg_hi[j].bitcast(F32),
                                        ALU.subtract).then_inc(merged_l, 1)

            def carry_kvu(c):
                dve.wait_ge(pv_done, count(c, UNITS, UNITS))
                dve.wait_ge(sum_step, count(c, 10, 10))
                for t in (k_hi, k_lo):
                    nc.vector.tensor_copy(t[:, 0:2 * P], t[:, T:T + 2 * P].bitcast(F32))\
                      .then_inc(kvu_moved, 1)
                for t in (v_hi, v_lo):
                    nc.vector.tensor_copy(t[:, 0:2, :], t[:, NB:NB + 2, :].bitcast(F32))\
                      .then_inc(kvu_moved, 1)
                nc.vector.tensor_copy(u[:, :, 0:FRESH], u[:, :, T:T + FRESH]).then_inc(kvu_moved, 1)

            def chunk(c):
                w = 0
                for t in HEAD_TILES:
                    evacuate(c, t)
                    split(c, w + SPLITS)
                    w += 1
                    if t == ("q", 1):
                        dve.wait_ge(v_hi_done, count(c, 1, 1))
                        nt = fresh(c) // P
                        ins = nc.vector.tensor_tensor(
                            v_lo[:, 2:2 + nt, :],
                            t_bank[0][:, 0:nt * P].rearrange("p (b f) -> p b f", f=P),
                            v_hi[:, 2:2 + nt, :].bitcast(F32), ALU.subtract)
                        if is_first(c):
                            ins = nc.vector.tensor_tensor(v_lo[:, 1, :], t_bank[1][:, 0:P],
                                                          v_hi[:, 1, :].bitcast(F32), ALU.subtract)
                        ins.then_inc(v_lo_done, 1)
                for s, tiles in enumerate(STEPS):
                    if s >= 2:
                        product(c, s - 2)
                    if s < UNITS:
                        maxima(c, s)
                    if s >= 3 and s % 2 == 1:
                        attention_lo(c, (s - 3) // 2)
                    if s >= 2 and s % 2 == 0:
                        pooled(c, s // 2 - 1)
                    if s:
                        pt_los(c, s - 1)
                    if s < UNITS:
                        normalise(c, s)
                    if s >= 2 and s % 2 == 0:
                        pooled_los(c, s // 2 - 1)
                    for t in tiles:
                        evacuate(c, t) if t[0] != "mix" else pool_out(c, t[1])
                        split(c, w + SPLITS)
                        w += 1
                product(c, UNITS - 1)
                attention_lo(c, NB - 1)
                for t in GATE_TILES:
                    if t[0] == "ab":
                        merge(c, t[1])
                    split(c, w + SPLITS)
                    w += 1
                    if t == ("ab", 2) and not is_last(c):
                        carry_kvu(c)
                for i in range(8):
                    if i == 0 and not is_last(c):
                        dve.wait_ge(tile_done, count(c, NW, INDEX[("ab", KD - 1)] + 1))
                        for t in (h_hi, h_lo):
                            nc.vector.tensor_copy(t[:, :, 0:P], t[:, :, T:T + P].bitcast(F32))\
                              .then_inc(h_moved, 1)
                    if i == 3 or i == 7:
                        for m in range(NB):
                            half = slice(0, T) if i == 3 else slice(T, D)
                            if m < NB - 1:
                                dve.wait_ge(out_done, count(c, 2 * (NB - 1), (i // 4) * (NB - 1) + m + 1))
                            else:
                                dve.wait_ge(tile_done, count(c, NW, w + 1))
                            dve.wait_ge(res_in[m], count(c, 1, 1, 16))
                            nc.vector.scalar_tensor_tensor(y[:, m, half], bank[m][:, :], 0.5,
                                                           y[:, m, half], ALU.mult, ALU.add)\
                              .then_inc(y_done, 1)
                    split(c, w + SPLITS)
                    w += 1
                    if not is_last(c):
                        if i in (0, 1):
                            rows_norm(c, NB, AHEAD + i + 1, (AHEAD + i) % 2)
                        if 2 <= i < 6:
                            rows_lo(c, NB, AHEAD + i - 1, P + (i - 2) * P)
                        if i in (3, 4):
                            rows_norm(c, NB, AHEAD + i, (AHEAD + i - 1) % 2)
                for m in range(NB):
                    dve.wait_ge(y_rstd, count(c, NB, m + 1))
                    if m == 0:
                        dve.wait_ge(s_const, 16 * N_CONST)
                    nc.vector.scalar_tensor_tensor(y[:, m, :], y[:, m, :], rstd[:, m:m + 1],
                                                   g_final[:, :], ALU.mult, ALU.mult).then_inc(y_norm, 1)

            over_chunks(dve, chunk)

        @block.tensor
        def _(pe):
            def passes(dst, a, b, start, stop):
                nc.tensor.matmul(dst, a[0], b[0], start=start, stop=False)
                nc.tensor.matmul(dst, a[0], b[1], start=False, stop=False)
                return nc.tensor.matmul(dst, a[1], b[0], start=False, stop=stop)

            def w_at(w, k):
                cols = slice(k * P, (k + 1) * P)
                return w_hi[:, w % SPLITS, cols], w_lo[:, w % SPLITS, cols]

            def h_at(k, lo, n):
                return h_hi[:, k, lo:lo + n], h_lo[:, k, lo:lo + n]

            def turn_rows(c, per, i, slot):
                pe.wait_ge(x_norm, count(c, per, i))
                pe.wait_ge(h_lo_done, count(c, per, i - 1))
                for k in range(KD):
                    ins = nc.tensor.transpose(bank[4 + k // 4][:, (k % 4) * P:(k % 4 + 1) * P],
                                              xn[:, slot, k * P:(k + 1) * P], ident[:, :])
                ins.then_inc(x_turned, 1)

            def dense(c, t, ks=range(KD)):
                kind, j = t
                w = INDEX[t]
                ahead = kind in ("k", "v", "u")
                n = fresh(c) if ahead else T
                at = P if ahead else 0
                dst = dense_bank(t)
                if ks[0] == 0:
                    i = DENSE.index(t)
                    pe.wait_ge(split_lo, count(c, NW, w + 1))
                    pe.wait_ge(*last_read(c, DENSE[i - 2], back=1 if i < 2 else 0))
                for k in ks:
                    ins = passes(dst[:, 0:n], w_at(w, k), h_at(k, at, n), k == 0, k == KD - 1)
                if ks[-1] == KD - 1:
                    if is_first(c) and ahead:
                        dst = {"k": bank[0], "v": bank[1], "u": pv_bank}[kind]
                        if kind == "u":
                            pe.wait_ge(prod_done, count(c, UNITS, 2 * j - 1))
                        for k in range(KD):
                            ins = passes(dst[:, 0:P], w_at(w, k), h_at(k, 0, P), k == 0, k == KD - 1)
                    ins.then_inc(tile_done, 1)

            def turn_v(c):
                pe.wait_ge(*last_read(c, ("v", 0)))
                pe.wait_ge(y_done, count(c, 8, 0))
                for b in range(fresh(c) // P):
                    ins = nc.tensor.transpose(t_bank[0][:, b * P:(b + 1) * P], v_t[:, b * P:(b + 1) * P],
                                              ident[:, :])
                if is_first(c):
                    ins = nc.tensor.transpose(t_bank[1][:, 0:P], v_t[:, T:T + P], ident[:, :])
                ins.then_inc(v_turned, 1)

            def scores(c, n):
                b, kv = divmod(n, 2)
                lo, hi = key_tiles(c, b)
                rows = slice(kv * HD, (kv + 1) * HD)
                keys = slice((b + lo) * P, (b + hi) * P)
                if n == 0:
                    pe.wait_ge(*last_read(c, ("q", 3)))
                for j in range(G):
                    pe.wait_ge(max_done, count(c, 4 * UNITS, 4 * n + j - 1))
                    queries = slice(b * P, (b + 1) * P)
                    passes(bank[j % 2][:, lo * P:hi * P],
                           (qa_hi[rows, j, queries], qa_lo[rows, j, queries]),
                           (k_hi[rows, keys], k_lo[rows, keys]), True, True).then_inc(qk_done, 1)

            def turn_p(c, n):
                lo, hi = key_tiles(c, n // 2)
                pe.wait_ge(norm_done, count(c, UNITS, n + 1))
                for kt in range(lo, hi):
                    pe.wait_ge(pt_lo_done, count(c, 3 * UNITS, 3 * (n - 1) + kt + 1))
                    for j in range(G):
                        ins = nc.tensor.transpose(t_bank[kt][:, j * P:(j + 1) * P],
                                                  p[:, n % 2, j, kt * P:(kt + 1) * P], ident[:, :])
                    ins.then_inc(pt_done, signals(lo, hi, kt))

            def values(c, n):
                b, kv = divmod(n, 2)
                lo, hi = key_tiles(c, b)
                pe.wait_ge(prod_done, count(c, UNITS, n))
                if is_first(c):
                    g = (n + 1) // 2
                    if g < NG:
                        pe.wait_ge(*last_read(c, ("u", g)))
                if n == 0:
                    pe.wait_ge(v_lo_done, count(c, 1, 1))
                for kt in range(lo, hi):
                    pe.wait_ge(pt_lo_done, count(c, 3 * UNITS, 3 * n + kt + 1))
                    ins = passes(pv_bank[:, :], (v_hi[:, b + kt, :], v_lo[:, b + kt, :]),
                                 (pt_hi[kt], pt_lo[kt]), kt == lo, kt == hi - 1)
                ins.then_inc(pv_done, 1)

            def mix(c, g):
                w = INDEX[("mix", g)]
                i = DENSE.index(("mix", g))
                pe.wait_ge(split_lo, count(c, NW, w + 1))
                pe.wait_ge(*last_read(c, DENSE[i - 2]))
                pe.wait_ge(pooled_l, count(c, NG, g + 1))
                passes(dense_bank(("mix", g))[:, :], w_at(w, 0), (pooled_hi, pooled_lo), True,
                       True).then_inc(tile_done, 1)

            def branches(c, j):
                w = INDEX[("ab", j)]
                pe.wait_ge(split_lo, count(c, NW, w + 1))
                if j == 0:
                    pe.wait_ge(at_lo_done, count(c, NB, NB))
                    pe.wait_ge(po_lo_done, count(c, NG, NG))
                else:
                    pe.wait_ge(gated, count(c, 2 * KD, 2 * (j - 1)))
                for a, (hi, lo) in enumerate(((qa_hi, qa_lo), (po_hi, po_lo))):
                    for k in range(4):
                        ins = passes(bank[2 * (j % 2) + a][:, :], w_at(w, 4 * a + k),
                                     (hi[:, k, :], lo[:, k, :]), k == 0, k == 3)
                ins.then_inc(tile_done, 1)

            def output(c, i):
                w = INDEX[("out", i)]
                half, pair = divmod(i, 4)
                pe.wait_ge(split_lo, count(c, NW, w + 1))
                if i == 0:
                    pe.wait_ge(merged_l, count(c, KD, KD))
                for m in range(NB):
                    if pair == 0 and half == 1:
                        pe.wait_ge(y_done, count(c, 8, m + 1))
                    for e in range(2):
                        k = 2 * pair + e
                        tok = slice(m * P, (m + 1) * P)
                        rhs = (w_hi[:, w % SPLITS, e * T:(e + 1) * T],
                               w_lo[:, w % SPLITS, e * T:(e + 1) * T])
                        ins = passes(bank[m][:, :], (mg_hi[k][:, tok], mg_lo[k][:, tok]), rhs,
                                     k == 0, k == KD - 1)
                    if pair == 3 and m < NB - 1:
                        ins.then_inc(out_done, 1)
                ins.then_inc(tile_done, 1)

            pe.wait_ge(s_made, 5)
            for i in range(AHEAD):
                turn_rows(0, 0, i + 1, i % 2)

            def chunk(c):
                if is_first(c):
                    pe.wait_ge(h_lo_done, AHEAD)
                else:
                    pe.wait_ge(h_lo_done, count(c, NB, AHEAD))
                for t in HEAD_TILES:
                    dense(c, t)
                    if t == ("q", 1):
                        turn_v(c)
                for s, tiles in enumerate(STEPS):
                    if s < UNITS:
                        scores(c, s)
                    dense(c, tiles[0], range(0, KD // 2))
                    if s:
                        turn_p(c, s - 1)
                    dense(c, tiles[0], range(KD // 2, KD))
                    if len(tiles) > 1:
                        mix(c, tiles[1][1])
                    if s:
                        values(c, s - 1)
                for t in GATE_TILES:
                    dense(c, t) if t[0] != "ab" else branches(c, t[1])
                for i in range(8):
                    output(c, i)
                    if 2 <= i < 6 and not is_last(c):
                        turn_rows(c, NB, AHEAD + i - 1, (AHEAD + i - 2) % 2)

            over_chunks(pe, chunk)


def kernel(x, norm_g, w_in, attn_sink, pool_w, pool_scale, w_branch_a, w_branch_b, w_out, final_norm_g):
    import numpy as np
    import concourse.bacc as bacc
    from concourse.bass_utils import run_bass_kernel_spmd

    def lay(a):
        return np.ascontiguousarray(a)

    heads = np.arange(NH * HD).reshape(2, G, HD).transpose(1, 0, 2).ravel()
    w = np.asarray(w_in)[0]
    off = np.cumsum([0, 512, 128, 128, 512, 512, 512, 1024, 1024])
    cols = np.concatenate([heads, np.arange(off[1], off[3]), off[3] + heads, np.arange(off[4], off[8])])
    w_in_t = lay(w[:, cols].reshape(KD, P, -1, P).transpose(2, 1, 0, 3).reshape(-1, P, D))
    ab = np.concatenate([np.asarray(w_branch_a)[0][heads], np.asarray(w_branch_b)[0]])
    w_ab_t = lay(ab.reshape(8, P, KD, P).transpose(2, 1, 0, 3).reshape(KD, P, D))
    w_out_t = lay(np.asarray(w_out)[0].reshape(4, 2, P, 2, T).transpose(3, 0, 2, 1, 4).reshape(8, P, D))
    arrays = {
        "in_x": lay(np.asarray(x)[0]), "in_w_in": w_in_t, "in_w_ab": w_ab_t, "in_w_out": w_out_t,
        "in_pool_w": lay(np.asarray(pool_w)[0]), "in_sink": lay(np.asarray(attn_sink)),
        "in_pool_scale": lay(np.asarray(pool_scale).reshape(NG, P)), "in_norm_g": lay(np.asarray(norm_g)),
        "in_final_g": lay(np.asarray(final_norm_g).reshape(1, D)),
    }
    nc = bacc.Bacc("TRN2", target_bir_lowering=False, num_devices=1)
    ap = {k: nc.dram_tensor(k, a.shape, mybir.dt.from_np(a.dtype), kind="ExternalInput").ap()
          for k, a in arrays.items()}
    out = nc.dram_tensor("out", (S, D), F32, kind="ExternalOutput").ap()
    build(nc, ap["in_x"], ap["in_w_in"], ap["in_w_ab"], ap["in_w_out"], ap["in_pool_w"], ap["in_sink"],
          ap["in_pool_scale"], ap["in_norm_g"], ap["in_final_g"], out)
    r = run_bass_kernel_spmd(nc, [arrays], core_ids=[0])
    return r.results[0]["out"].reshape(1, S, D)
```

```python
from contextlib import ExitStack

import concourse.bass as bass
from concourse import mybir

F32 = mybir.dt.float32
F32R = mybir.dt.float32r
BF16 = mybir.dt.bfloat16
ALU = mybir.AluOpType
ACT = mybir.ActivationFunctionType

P = 128
D = 1024
S = 4096
HD = 64
NH = 8
G = 4
WINDOWS = (2, 4, 8, 16)
NG = len(WINDOWS)
EPS = 1e-6
MASKED = -1e30
T = 512
NB = T // P
CHUNKS = S // T
LAST = CHUNKS - 1
KD = D // P
HW = T + P
KW = T + 2 * P
LEFT = 8
UW = LEFT + HW
FRESH = LEFT + P
UNITS = 2 * NB

HEAD_TILES = [("k", 0), ("v", 0)] + [("q", j) for j in range(4)] + [("za", j) for j in range(4)]
STEPS = [[("u", 0)], [("zb", 0)], [("u", 1)], [("mix", 0), ("zb", 1)], [("u", 2)],
         [("mix", 1), ("zb", 2)], [("u", 3)], [("mix", 2), ("zb", 3)], [("ga", 0)]]
GATE_TILES = [("gb", 0), ("mix", 3)] + [(k, j) for j in range(KD) for k in ("ga", "gb", "ab")][2:]
OUT_TILES = [("out", i) for i in range(8)]
TILES = HEAD_TILES + [t for s in STEPS for t in s] + GATE_TILES + OUT_TILES
NW = len(TILES)
SPLITS = 3
RAWS = 2
INDEX = {t: w for w, t in enumerate(TILES)}
DENSE = [t for t in TILES if t[0] not in ("mix", "ab", "out")]
DVE_LAST = [t for t in DENSE if t[0] in ("k", "q", "za", "zb")]
ACT_LAST = [t for t in DENSE if t[0] in ("v", "u", "ga", "gb")]
assert NW % SPLITS == 0 and NW % RAWS == 0 and len(DENSE) % 2 == 0


def cols_of(kind):
    return P if kind == "mix" else D


def build(nc, x, w_in_t, w_ab_t, w_out_t, pool_w, attn_sink, pool_scale, norm_g, final_g, out):
    with ExitStack() as ctx:
        def sb(name, shape, dt=F32):
            return ctx.enter_context(nc.sbuf_tensor(name, shape, dt))

        def sem(name):
            return ctx.enter_context(nc.semaphore(name))

        h_hi = sb("h_hi", [P, KD, HW], F32R)
        h_lo = sb("h_lo", [P, KD, HW], F32R)
        qa = [sb(f"qa{kv}", [P, 4, T], F32R) for kv in range(2)]
        po_hi = sb("po_hi", [P, NG, T], F32R)
        po_lo = sb("po_lo", [P, NG, T], F32R)
        arena_r = sb("arena_r", [P, 8 * 2 * T], F32R)
        arena_f = sb("arena_f", [P, 6 * D])
        k_hi = [sb(f"k_hi{kv}", [P, KW], F32R) for kv in range(2)]
        k_lo = sb("k_lo", [P, KW], F32R)
        v = sb("v", [P, KW // P, 2, 2, HD], F32R)
        u = sb("u", [P, NG, UW])
        sums = sb("sums", [P, 2, T + 16])
        raw = sb("raw", [P, RAWS, D])
        w_hi = sb("w_hi", [P, SPLITS, D], F32R)
        w_lo = sb("w_lo", [P, SPLITS, D], F32R)
        bias = sb("bias", [P, NH, 3 * P], BF16)
        g_norm = sb("g_norm", [P, D])
        g_final = sb("g_final", [P, D])
        ident = sb("ident", [P, P])
        eps = sb("eps", [P, 1])
        minus_half = sb("minus_half", [P, 1])
        recip = sb("recip", [P, 16])
        recip_down = sb("recip_down", [P, 16])
        sink = sb("sink", [P, NH])
        minus_sink = sb("minus_sink", [P, NH])
        half_scale = sb("half_scale", [P, NG])
        row_max = sb("row_max", [P, 2, G])
        minus_max = sb("minus_max", [P, 2, G])
        row_sum = sb("row_sum", [P, 2, G])
        sink_term = sb("sink_term", [P, 2, G])
        waiter = sb("waiter", [P, 2, G])
        ssq = sb("ssq", [P, 9])
        ms = sb("ms", [P, 9])
        rstd = sb("rstd", [P, 9])

        v_t = arena_f[:, 0:HW]
        p = arena_f[:, 0:2 * G * 3 * P].rearrange("p (b h k) -> p b h k", b=2, h=G)
        za = arena_f[:, 3 * D:5 * D].rearrange("p (j t) -> p j t", j=4)
        zb = arena_f[:, 5 * D:6 * D].rearrange("p (j t) -> p j t", j=2)
        gate = arena_f[:, 0:2 * D].rearrange("p (b a t) -> p b a t", b=2, a=2)
        xn = arena_f[:, :].rearrange("p (b f) -> p b f", b=6)
        y = arena_f[:, 2 * D:6 * D].rearrange("p (m f) -> p m f", m=NB)
        prod = sb("prod", [P, G, P])
        junk = sums[:, :, :].rearrange("p a b -> p (a b)").bitcast(BF16)[:, 0:D]
        pt_hi = [arena_r[:, kt * 2 * T:kt * 2 * T + T] for kt in range(3)]
        pt_lo = [arena_r[:, kt * 2 * T + T:(kt + 1) * 2 * T] for kt in range(3)]
        pooled_hi = arena_r[:, 6 * T:7 * T]
        pooled_lo = arena_r[:, 7 * T:8 * T]
        mg_hi = [arena_r[:, j * 2 * T:j * 2 * T + T] for j in range(KD)]
        mg_lo = [arena_r[:, j * 2 * T + T:(j + 1) * 2 * T] for j in range(KD)]

        bank = [ctx.enter_context(nc.psum_tensor(f"bank{i}", [P, T], F32)) for i in range(8)]
        mix_bank, pv_bank, t_bank = bank[1], bank[2], bank[3:6]
        u_bank = t_bank[2]

        gain_in = sem("gain_in")
        s_const = sem("s_const")
        s_made = sem("s_made")
        s_abs = sem("s_abs")
        s_cdve = sem("s_cdve")
        raw_in = [sem(f"raw_in{i}") for i in range(RAWS)]
        split_hi = sem("split_hi")
        split_lo = sem("split_lo")
        tile_done = sem("tile_done")
        act_read = sem("act_read")
        dve_read = sem("dve_read")
        hi_kq = sem("hi_kq")
        mix_read = sem("mix_read")
        tanh_z = sem("tanh_z")
        v_turned = sem("v_turned")
        v_hi_done = sem("v_hi_done")
        v_lo_done = sem("v_lo_done")
        qk_done = sem("qk_done")
        max_done = sem("max_done")
        neg_done = sem("neg_done")
        sink_in = sem("sink_in")
        exp_done = sem("exp_done")
        den_done = sem("den_done")
        norm_done = sem("norm_done")
        norm_act = sem("norm_act")
        pt_done = sem("pt_done")
        pt_hi_done = sem("pt_hi_done")
        pt_lo_done = sem("pt_lo_done")
        pv_done = sem("pv_done")
        low_read = sem("low_read")
        pv_read = sem("pv_read")
        prod_done = sem("prod_done")
        at_hi_done = sem("at_hi_done")
        at_lo_done = sem("at_lo_done")
        sum_step = sem("sum_step")
        pooled_f = sem("pooled_f")
        edge_done = sem("edge_done")
        pooled_h = sem("pooled_h")
        pooled_l = sem("pooled_l")
        po_hi_done = sem("po_hi_done")
        po_lo_done = sem("po_lo_done")
        gated = sem("gated")
        merged_f = sem("merged_f")
        merged_h = sem("merged_h")
        merged_l = sem("merged_l")
        kvu_moved = sem("kvu_moved")
        h_moved = sem("h_moved")
        x_first = [sem(f"x_first{i}") for i in range(NB + 1)]
        x_in = [sem(f"x_in{i}") for i in range(2)]
        x_sq = sem("x_sq")
        x_ms = sem("x_ms")
        x_rstd = sem("x_rstd")
        x_norm = sem("x_norm")
        x_turned = sem("x_turned")
        h_hi_done = sem("h_hi_done")
        h_lo_done = sem("h_lo_done")
        res_in = [sem(f"res_in{m}") for m in range(NB)]
        out_done = sem("out_done")
        y_done = sem("y_done")
        y_sq = sem("y_sq")
        y_ms = sem("y_ms")
        y_rstd = sem("y_rstd")
        y_norm = sem("y_norm")
        stored = [sem(f"stored{m}") for m in range(NB)]

        N_CONST = 3
        AHEAD = NB + 1

        def count(c, per, i, unit=1):
            value = (c * per + i) * unit
            return max(value, 0) if isinstance(c, int) else value

        def last_read(c, t, back=0):
            if t in DVE_LAST:
                return dve_read, count(c, len(DVE_LAST), DVE_LAST.index(t) + 1 - back * len(DVE_LAST))
            return act_read, count(c, len(ACT_LAST), ACT_LAST.index(t) + 1 - back * len(ACT_LAST))

        def dense_bank(t):
            return bank[6 + DENSE.index(t) % 2]

        def fresh(c):
            return T - P if is_last(c) else T

        def is_first(c):
            return isinstance(c, int) and c == 0

        def is_last(c):
            return isinstance(c, int) and c == LAST

        def key_tiles(c, b):
            lo = 1 if is_first(c) and b == 0 else 0
            hi = 2 if is_last(c) and b == NB - 1 else 3
            return lo, hi

        def over_chunks(eng, chunk):
            chunk(0)
            with eng.Fori(1, LAST) as c:
                chunk(c)
            chunk(LAST)

        def signals(lo, hi, kt):
            return 2 if (lo == 1 and kt == 1) or (hi == 2 and kt == 1) else 1

        def pooled_at(g):
            return sums[:, 1 - g % 2, 0:T]

        block = ctx.enter_context(nc.Block())

        @block.sync
        def _(sp):
            def load_weight(c, w):
                kind, j = TILES[w]
                n = cols_of(kind)
                at = {"q": 0, "k": 4, "v": 5, "za": 6, "u": 10, "zb": 14, "ga": 18, "gb": 26}
                src = (pool_w[j] if kind == "mix" else w_ab_t[j] if kind == "ab" else
                       w_out_t[j] if kind == "out" else w_in_t[at[kind] + j])
                sp.wait_ge(split_lo, count(c, NW, w + 1 - RAWS))
                sp.dma_start(raw[:, w % RAWS, 0:n], src).then_inc(raw_in[w % RAWS], 16)

            def load_rows(c, m):
                if m < 2:
                    sp.wait_ge(merged_l, count(c, KD, KD))
                else:
                    sp.wait_ge(x_turned, count(c, NB, AHEAD + m - 1))
                slot = m % 2
                tile = (c * NB + AHEAD + m) % (S // P)
                sp.dma_start(xn[:, slot, :], x[bass.ds(tile * P, P), :]).then_inc(x_in[slot], 16)

            def chunk(c):
                for w in range(NW):
                    if w == INDEX[("ga", 2)]:
                        sp.wait_ge(pt_done, count(c, 3 * UNITS, 3 * UNITS))
                        sp.wait_ge(prod_done, count(c, NB, NB))
                        sp.wait_ge(po_lo_done, count(c, NG, NG))
                        for m in range(NB):
                            sp.dma_start(y[:, m, :], x[bass.ds(c * T + m * P, P), :])\
                              .then_inc(res_in[m], 16)
                    if not is_last(c):
                        if w == INDEX[("out", 4)]:
                            load_rows(c, 0)
                            load_rows(c, 1)
                        if w == INDEX[("out", 7)]:
                            load_rows(c, 2)
                    if not (is_first(c) and w < RAWS):
                        load_weight(c, w)
                if not is_last(c):
                    load_rows(c, 3)

            for i in range(AHEAD):
                sp.dma_start(xn[:, i, :], x[i * P:(i + 1) * P, :]).then_inc(x_first[i], 16)
            for w in range(RAWS):
                load_weight(0, w)
            over_chunks(sp, chunk)
            for m in range(NB):
                sp.wait_ge(stored[m], 16 * CHUNKS)

        @block.gpsimd
        def _(pool):
            nc.gpsimd.memset(ident[:, :], 0.0).then_inc(s_made, 1)
            nc.gpsimd.memset(eps[:, :], EPS).then_inc(s_made, 1)
            nc.gpsimd.memset(minus_half[:, :], -0.5).then_inc(s_made, 1)
            nc.gpsimd.memset(u[:, :, 0:LEFT], 0.0).then_inc(s_made, 1)
            pool.wait_ge(s_made, 4)
            nc.gpsimd.affine_select(out=ident[:, :], in_=ident[:, :], compare_op=ALU.not_equal, fill=1.0,
                                    base=0, pattern=[[-1, P]], channel_multiplier=1).then_inc(s_made, 1)

            def rstd_of(c, per, i, col, sq, ms_sem, rs_sem):
                pool.wait_ge(sq, count(c, per, i))
                nc.gpsimd.tensor_tensor(ms[:, col:col + 1], ssq[:, col:col + 1], eps[:, :],
                                        ALU.add).then_inc(ms_sem, 1)
                pool.wait_ge(ms_sem, count(c, per, i))
                nc.gpsimd.tensor_tensor(rstd[:, col:col + 1], ms[:, col:col + 1], minus_half[:, :],
                                        ALU.pow).then_inc(rs_sem, 1)

            for i in range(2):
                rstd_of(0, 0, i + 1, 4 + i, x_sq, x_ms, x_rstd)
            dist = arena_f[:, 5 * D:5 * D + 3 * P]
            nc.gpsimd.iota(dist, pattern=[[-1, 3 * P]], base=P, channel_multiplier=1,
                           allow_small_or_imprecise_dtypes=True).then_inc(s_made, 1)
            nc.gpsimd.iota(recip[:, :], pattern=[[1, 16]], base=1, channel_multiplier=0,
                           allow_small_or_imprecise_dtypes=True).then_inc(s_made, 1)
            nc.gpsimd.iota(recip_down[:, :], pattern=[[-1, 16]], base=16, channel_multiplier=0,
                           allow_small_or_imprecise_dtypes=True).then_inc(s_made, 1)
            for i in range(2, AHEAD):
                rstd_of(0, 0, i + 1, 4 + i, x_sq, x_ms, x_rstd)
            pool.wait_ge(s_cdve, 8)
            nc.gpsimd.affine_select(out=bias[:, :, :], in_=bias[:, :, :], compare_op=ALU.is_ge, fill=MASKED,
                                    base=0, pattern=[[0, NH], [1, 3 * P]], channel_multiplier=-1)\
                     .then_inc(s_made, 1)
            pool.wait_ge(s_made, 9)
            nc.gpsimd.affine_select(out=bias[:, :, :], in_=bias[:, :, :], compare_op=ALU.is_ge, fill=MASKED,
                                    base=2 * P, pattern=[[0, NH], [-1, 3 * P]], channel_multiplier=1)\
                     .then_inc(s_made, 1)

            def window_sums(c, g):
                win = WINDOWS[g]
                a = LEFT - win // 2
                step, width, src = 1, T + win - 2, u[:, g, a:a + T + win - 1]
                pool.wait_ge(*last_read(c, ("u", g)))
                if g:
                    pool.wait_ge(pooled_l, count(c, NG, g))
                else:
                    pool.wait_ge(y_sq, count(c, NB, 0))
                    pool.wait_ge(pooled_l, count(c, NG, 0))
                which, done = 0, g * (g + 1) // 2
                while True:
                    dst = sums[:, which, 0:width]
                    if step > 1:
                        pool.wait_ge(sum_step, count(c, 10, done))
                    nc.gpsimd.tensor_tensor(dst, src[:, 0:width], src[:, step:step + width],
                                            ALU.add).then_inc(sum_step, 1)
                    done += 1
                    step *= 2
                    if step == win:
                        break
                    src, which, width = sums[:, which, :], 1 - which, width - step

            def gate_output(c, b):
                pool.wait_ge(pv_read, count(c, UNITS, 2 * b + 2))
                nc.gpsimd.tensor_tensor(prod[:, :, :], prod[:, :, :], za[:, :, b * P:(b + 1) * P],
                                        ALU.mult).then_inc(prod_done, 1)

            def attention_lo(c, b):
                pool.wait_ge(at_hi_done, count(c, NB, b + 1))
                nc.gpsimd.tensor_tensor(qa[1][:, :, b * P:(b + 1) * P], prod[:, :, :],
                                        qa[0][:, :, b * P:(b + 1) * P].bitcast(F32),
                                        ALU.subtract).then_inc(at_lo_done, 1)

            def pooled_lo_of(c, g):
                pool.wait_ge(pooled_h, count(c, NG, g + 1))
                nc.gpsimd.tensor_tensor(pooled_lo, pooled_at(g), pooled_hi.bitcast(F32),
                                        ALU.subtract).then_inc(pooled_l, 1)

            def pool_out_lo(c, g):
                pool.wait_ge(po_hi_done, count(c, NG, g + 1))
                nc.gpsimd.tensor_tensor(po_lo[:, g, :], zb[:, g % 2, :], po_hi[:, g, :].bitcast(F32),
                                        ALU.subtract).then_inc(po_lo_done, 1)

            def chunk(c):
                if is_last(c):
                    pool.wait_ge(kvu_moved, 5 * LAST)
                    end = LEFT + T
                    nc.gpsimd.memset(u[:, :, end:end + LEFT], 0.0).then_inc(s_made, 1)
                    pool.wait_ge(s_made, 11)
                for s in range(1, len(STEPS)):
                    if s >= 3 and s % 2 == 1:
                        attention_lo(c, (s - 3) // 2)
                    if s % 2 == 1 and s // 2 < NG:
                        window_sums(c, s // 2)
                    if s >= 4 and s % 2 == 0:
                        pool_out_lo(c, (s - 4) // 2)
                    if s % 2 == 0:
                        gate_output(c, s // 2 - 1)
                        pooled_lo_of(c, s // 2 - 1)
                attention_lo(c, NB - 1)
                pool_out_lo(c, NG - 1)
                if not is_last(c):
                    for m in range(NB):
                        rstd_of(c, NB, AHEAD + m + 1, 4 + m % 2, x_sq, x_ms, x_rstd)
                for m in range(NB):
                    rstd_of(c, NB, m + 1, m, y_sq, y_ms, y_rstd)

            over_chunks(pool, chunk)

        @block.scalar
        def _(act):
            def split(c, w):
                if w >= NW and is_last(c):
                    return
                n = cols_of(TILES[w % NW][0])
                act.wait_ge(raw_in[w % RAWS], count(c, NW // RAWS, w // RAWS + 1, 16))
                act.wait_ge(tile_done, count(c, NW, w - SPLITS + 1))
                nc.scalar.activation(w_hi[:, w % SPLITS, 0:n], raw[:, w % RAWS, 0:n],
                                     ACT.Copy).then_inc(split_hi, 1)

            def rows_square(c, per, i, slot):
                if per:
                    m = i - AHEAD - 1
                    act.wait_ge(x_in[slot], count(c, 2, m // 2 + 1, 16))
                    act.wait_ge(x_ms, count(c, per, i - 2))
                else:
                    act.wait_ge(x_first[slot], 16)
                act.wait_ge(x_sq, count(c, per, i - 1))
                nc.scalar.activation(junk, xn[:, slot, :], ACT.Square, scale=D ** -0.5,
                                     accum_out=ssq[:, 4 + slot:5 + slot]).then_inc(x_sq, 1)

            def rows_hi(c, per, i, at, b=4):
                act.wait_ge(x_turned, count(c, per, i))
                for half in range(2):
                    ins = nc.scalar.activation(
                        h_hi[:, 4 * half:4 * half + 4, at:at + P],
                        bank[b + half][:, :].rearrange("p (k t) -> p k t", k=4), ACT.Copy)
                ins.then_inc(h_hi_done, 1)

            act.dma_start(g_norm[:, :], norm_g.to_broadcast([P, D])).then_inc(gain_in, 16)
            act.dma_start(sink[:, :], attn_sink.to_broadcast([P, NH])).then_inc(s_const, 16)
            with nc.allow_non_contiguous_dma("512 values, once"):
                act.dma_start(half_scale[:, :], pool_scale.rearrange("g p -> p g")).then_inc(s_const, 16)
            for i in range(AHEAD + 2):
                if i < AHEAD:
                    rows_square(0, 0, i + 1, i)
                if i >= 2:
                    rows_hi(0, 0, i - 1, (i - 2) * P, 2 * ((i - 2) % 4))
                if i == AHEAD:
                    split(0, 0)
                if i == 2:
                    act.dma_start(g_final[:, :], final_g.to_broadcast([P, D])).then_inc(s_const, 16)
                    act.wait_ge(s_made, 6)
                    dist = arena_f[:, 5 * D:5 * D + 3 * P]
                    nc.scalar.activation(dist, dist, ACT.Abs).then_inc(s_abs, 1)
            for w in range(1, SPLITS):
                split(0, w)

            def evacuate(c, t):
                kind, j = t
                src = dense_bank(t)
                act.wait_ge(tile_done, count(c, NW, INDEX[t] + 1))
                n = fresh(c)
                if kind == "k":
                    act.wait_ge(kvu_moved, count(c, 5, 0))
                    for kv in range(2):
                        rows = slice(kv * HD, (kv + 1) * HD)
                        for to in (slice(0, HD), slice(HD, P)):
                            ins = nc.scalar.activation(k_hi[kv][to, 2 * P:2 * P + n], src[rows, 0:n],
                                                       ACT.Copy)
                            if is_first(c):
                                ins = nc.scalar.activation(k_hi[kv][to, P:2 * P], bank[0][rows, 0:P],
                                                           ACT.Copy)
                    ins.then_inc(hi_kq, 1)
                elif kind == "v":
                    ins = nc.scalar.activation(v_t[:, 0:n], src[:, 0:n], ACT.Copy)
                    if is_first(c):
                        ins = nc.scalar.activation(v_t[:, T:T + P], bank[1][:, 0:P], ACT.Copy)
                    ins.then_inc(act_read, 1)
                elif kind == "q":
                    act.wait_ge(tile_done, count(c, NW, INDEX[("ab", KD - 1)] + 1 - NW))
                    for kv in range(2):
                        rows = slice(kv * HD, (kv + 1) * HD)
                        ins = nc.scalar.activation(qa[kv][rows, j, :], src[rows, :], ACT.Copy,
                                                   scale=HD ** -0.5)
                    ins.then_inc(hi_kq, 1)
                elif kind == "za":
                    if j == 0:
                        for m in range(NB):
                            act.wait_ge(stored[m], count(c, 1, 0, 16))
                    nc.scalar.activation(za[:, j, :], src[:, :], ACT.Tanh, scale=0.5).then_inc(tanh_z, 1)
                elif kind == "zb":
                    if j >= 2:
                        act.wait_ge(po_lo_done, count(c, NG, j - 1))
                    nc.scalar.activation(zb[:, j % 2, :], src[:, :], ACT.Tanh, scale=0.5)\
                      .then_inc(tanh_z, 1)
                elif kind == "u":
                    act.wait_ge(kvu_moved, count(c, 5, 0))
                    ins = nc.scalar.activation(u[:, j, FRESH:FRESH + n], src[:, 0:n], ACT.Copy)
                    if is_first(c):
                        ins = nc.scalar.activation(u[:, j, LEFT:FRESH], u_bank[:, 0:P], ACT.Copy)
                    ins.then_inc(act_read, 1)
                elif kind in ("ga", "gb"):
                    if j < 2:
                        act.wait_ge(pt_done, count(c, 3 * UNITS, 3 * UNITS))
                    else:
                        act.wait_ge(merged_l, count(c, KD, j - 1))
                    nc.scalar.activation(gate[:, j % 2, "ab".index(kind[1]), :], src[:, :], ACT.Tanh,
                                         scale=0.5).then_inc(act_read, 1)

            def exps(c, n):
                b, kv = divmod(n, 2)
                lo, hi = key_tiles(c, b)
                act.wait_ge(neg_done, count(c, UNITS, n + 1))
                for j in range(G):
                    pj = p[:, n % 2, j, lo * P:hi * P]
                    nc.scalar.activation(pj, pj, ACT.Exp, bias=minus_max[:, n % 2, j:j + 1],
                                         accum_out=row_sum[:, n % 2, j:j + 1])
                act.wait_ge(sink_in, count(c, UNITS, n + 1))
                nc.scalar.activation(sink_term[:, n % 2, :], sink_term[:, n % 2, :],
                                     ACT.Exp).then_inc(exp_done, 1)

            def pt_his(c, n):
                lo, hi = key_tiles(c, n // 2)
                for kt in range(lo, hi):
                    act.wait_ge(pt_done, count(c, 3 * UNITS, 3 * n + kt + 1))
                    act.wait_ge(pv_done, count(c, UNITS, n))
                    nc.scalar.activation(pt_hi[kt], t_bank[kt][:, :], ACT.Copy)\
                      .then_inc(pt_hi_done, signals(lo, hi, kt))

            def take_low(c, n):
                b, kv = divmod(n, 2)
                act.wait_ge(pv_done, count(c, UNITS, n + 1))
                act.wait_ge(at_lo_done, count(c, NB, b))
                nc.scalar.activation(prod[kv * HD:(kv + 1) * HD, :, :],
                                     pv_bank[HD:P, :].rearrange("p (j q) -> p j q", j=G),
                                     ACT.Copy, scale=0.5).then_inc(low_read, 1)

            def normalise(c, n):
                lo, hi = key_tiles(c, n // 2)
                act.wait_ge(den_done, count(c, 2 * UNITS, 2 * n + 2))
                for j in range(2, G):
                    pj = p[:, n % 2, j, lo * P:hi * P]
                    ins = nc.scalar.activation(pj, pj, ACT.Copy, scale=row_sum[:, n % 2, j:j + 1])
                ins.then_inc(norm_act, 1)

            def v_hi_of(c):
                nt = fresh(c) // P
                act.wait_ge(v_turned, count(c, 1, 1))
                act.wait_ge(kvu_moved, count(c, 5, 0))
                ins = nc.scalar.activation(
                    v[:, 2:2 + nt, :, 0, :],
                    t_bank[0][:, 0:nt * P].rearrange("p (b v f) -> p b v f", v=2, f=HD), ACT.Copy)
                if is_first(c):
                    ins = nc.scalar.activation(
                        v[:, 1, :, 0, :], t_bank[1][:, 0:P].rearrange("p (v f) -> p v f", v=2), ACT.Copy)
                ins.then_inc(v_hi_done, 1)

            def merge_hi(c, j):
                act.wait_ge(merged_f, count(c, KD, j + 1))
                nc.scalar.activation(mg_hi[j], gate[:, j % 2, 0, :], ACT.Copy).then_inc(merged_h, 1)

            def attention_hi(c, b):
                act.wait_ge(prod_done, count(c, NB, b + 1))
                nc.scalar.activation(qa[0][:, :, b * P:(b + 1) * P], prod[:, :, :],
                                     ACT.Copy).then_inc(at_hi_done, 1)

            def pooled_his(c, g):
                act.wait_ge(pooled_f, count(c, NG, g + 1))
                act.wait_ge(tile_done, count(c, NW, INDEX[("mix", g - 1)] + 1 if g else 0))
                nc.scalar.activation(pooled_hi, pooled_at(g), ACT.Copy).then_inc(pooled_h, 1)

            def pool_out_hi(c, g):
                act.wait_ge(mix_read, count(c, NG, g + 1))
                nc.scalar.activation(po_hi[:, g, :], zb[:, g % 2, :], ACT.Copy).then_inc(po_hi_done, 1)

            def finish(c, tiles):
                for t in sorted(tiles, key=lambda t: t[0] != "mix"):
                    if t[0] == "mix":
                        pool_out_hi(c, t[1])
                    elif t[0] == "ab":
                        merge_hi(c, t[1])
                    elif t[0] != "out":
                        evacuate(c, t)
                for t in tiles:
                    split(c, INDEX[t] + SPLITS)

            def store(c):
                for m in range(NB):
                    act.wait_ge(y_norm, count(c, NB, m + 1 - NB))
                    act.dma_start(out[bass.ds(c * T - T + m * P, P), :], y[:, m, :])\
                       .then_inc(stored[m], 16)

            def chunk(c):
                for t in HEAD_TILES[:-1]:
                    finish(c, [t])
                    if t == ("v", 0) and not is_first(c):
                        store(c)
                    if t == ("q", 1):
                        v_hi_of(c)
                for s, tiles in enumerate(STEPS):
                    finish(c, STEPS[s - 1] if s else HEAD_TILES[-1:])
                    if s:
                        pt_his(c, s - 1)
                    if s >= 3 and s % 2 == 1:
                        attention_hi(c, (s - 3) // 2)
                    if s < UNITS:
                        exps(c, s)
                    if s:
                        take_low(c, s - 1)
                    if s < UNITS:
                        normalise(c, s)
                    if s >= 2 and s % 2 == 0:
                        pooled_his(c, s // 2 - 1)
                finish(c, STEPS[-1])
                attention_hi(c, NB - 1)
                finish(c, GATE_TILES[:2])
                for t in GATE_TILES[2:]:
                    finish(c, [t])
                w = INDEX[("out", 0)]
                for i in range(8):
                    split(c, w + SPLITS)
                    w += 1
                    if not is_last(c):
                        if 2 <= i < 6:
                            if i == 2:
                                act.wait_ge(h_moved, count(c, 2, 2))
                            rows_hi(c, NB, AHEAD + i - 1, P + (i - 2) * P)
                        if i in (0, 1, 3, 4):
                            m = (0, 1, None, 2, 3)[i]
                            rows_square(c, NB, AHEAD + m + 1, m % 2)
                for m in range(NB):
                    act.wait_ge(y_done, count(c, 8, NB + m + 1))
                    act.wait_ge(y_sq, count(c, NB, m))
                    nc.scalar.activation(junk, y[:, m, :], ACT.Square, scale=D ** -0.5,
                                         accum_out=ssq[:, m:m + 1]).then_inc(y_sq, 1)

            over_chunks(act, chunk)
            store(CHUNKS)

        @block.vector
        def _(dve):
            def split(c, w):
                if w >= NW and is_last(c):
                    return
                n = cols_of(TILES[w % NW][0])
                dve.wait_ge(split_hi, count(c, NW, w + 1))
                nc.vector.tensor_tensor(w_lo[:, w % SPLITS, 0:n], raw[:, w % RAWS, 0:n],
                                        w_hi[:, w % SPLITS, 0:n].bitcast(F32),
                                        ALU.subtract).then_inc(split_lo, 1)

            def rows_norm(c, per, i, slot):
                dve.wait_ge(x_rstd, count(c, per, i))
                nc.vector.scalar_tensor_tensor(xn[:, slot, :], xn[:, slot, :], rstd[:, 4 + slot:5 + slot],
                                               g_norm[:, :], ALU.mult, ALU.mult).then_inc(x_norm, 1)

            def rows_lo(c, per, i, at, b=4):
                dve.wait_ge(h_hi_done, count(c, per, i))
                for half in range(2):
                    ks = slice(4 * half, 4 * half + 4)
                    ins = nc.vector.tensor_tensor(
                        h_lo[:, ks, at:at + P], bank[b + half][:, :].rearrange("p (k t) -> p k t", k=4),
                        h_hi[:, ks, at:at + P].bitcast(F32), ALU.subtract)
                ins.then_inc(h_lo_done, 1)

            dve.wait_ge(gain_in, 16)
            for i in range(AHEAD + 2):
                if i < AHEAD:
                    rows_norm(0, 0, i + 1, i)
                if i >= 2:
                    rows_lo(0, 0, i - 1, (i - 2) * P, 2 * ((i - 2) % 4))
            for w in range(SPLITS):
                split(0, w)
            dve.wait_ge(s_const, 16 * N_CONST)
            dve.wait_ge(s_abs, 1)
            dist = arena_f[:, 5 * D:5 * D + 3 * P]
            for hd in range(NH):
                nc.vector.tensor_scalar(bias[:, hd, :], dist, -(2.0 ** -(hd + 1)), None,
                                        ALU.mult).then_inc(s_cdve, 1)
            nc.vector.tensor_scalar(minus_sink[:, :], sink[:, :], -1.0, None, ALU.mult).then_inc(s_cdve, 1)
            nc.vector.tensor_scalar(half_scale[:, :], half_scale[:, :], 0.5, None,
                                    ALU.mult).then_inc(s_cdve, 1)
            dve.wait_ge(s_made, 8)
            nc.vector.reciprocal(recip[:, :], recip[:, :]).then_inc(s_cdve, 1)
            nc.vector.reciprocal(recip_down[:, :], recip_down[:, :]).then_inc(s_cdve, 1)
            dve.wait_ge(s_cdve, 8 + 4)
            dve.wait_ge(s_made, 10)

            def evacuate(c, t):
                kind, j = t
                src = dense_bank(t)
                n = fresh(c)
                if kind == "k":
                    dve.wait_ge(hi_kq, count(c, 5, 1))
                    for kv in range(2):
                        rows = slice(kv * HD, (kv + 1) * HD)
                        ins = nc.vector.tensor_tensor(
                            k_lo[rows, 2 * P:2 * P + n], src[rows, 0:n],
                            k_hi[kv][rows, 2 * P:2 * P + n].bitcast(F32), ALU.subtract)
                        if is_first(c):
                            ins = nc.vector.tensor_tensor(
                                k_lo[rows, P:2 * P], bank[0][rows, 0:P],
                                k_hi[kv][rows, P:2 * P].bitcast(F32), ALU.subtract)
                    ins.then_inc(dve_read, 1)
                elif kind == "q":
                    dve.wait_ge(hi_kq, count(c, 5, j + 2))
                    for kv in range(2):
                        rows, to = slice(kv * HD, (kv + 1) * HD), slice((1 - kv) * HD, (2 - kv) * HD)
                        ins = nc.vector.scalar_tensor_tensor(
                            qa[kv][to, j, :], src[rows, :], HD ** -0.5, qa[kv][rows, j, :].bitcast(F32),
                            ALU.mult, ALU.subtract)
                    ins.then_inc(dve_read, 1)
                elif kind in ("za", "zb"):
                    dst = za[:, j, :] if kind == "za" else zb[:, j % 2, :]
                    dve.wait_ge(tanh_z, count(c, 8, (0 if kind == "za" else 4) + j + 1))
                    nc.vector.scalar_tensor_tensor(dst, dst, 1.0, src[:, :], ALU.add,
                                                   ALU.mult).then_inc(dve_read, 1)

            def maxima(c, n):
                b, kv = divmod(n, 2)
                lo, hi = key_tiles(c, b)
                for j in range(G):
                    dve.wait_ge(qk_done, count(c, 4 * UNITS, 4 * n + j + 1))
                    if j == 0:
                        dve.wait_ge(pt_done, count(c, 3 * UNITS, 3 * (n - 1)))
                    nc.vector.memset(waiter[:, n % 2, j:j + 1], 0.0)
                    nc.vector.tensor_tensor_reduce(
                        p[:, n % 2, j, lo * P:hi * P], bank[j % 2][:, lo * P:hi * P],
                        bias[:, kv * G + j, lo * P:hi * P], 1.0, -3.0e38, ALU.add, ALU.max,
                        row_max[:, n % 2, j:j + 1]).then_inc(max_done, 1)
                dve.wait_ge(max_done, count(c, 4 * UNITS, 4 * n + 4))
                nc.vector.scalar_tensor_tensor(minus_max[:, n % 2, :], row_max[:, n % 2, :], -1.0,
                                               minus_sink[:, kv * G:kv * G + G], ALU.mult,
                                               ALU.min).then_inc(neg_done, 1)
                dve.wait_ge(neg_done, count(c, UNITS, n + 1))
                nc.vector.tensor_tensor(sink_term[:, n % 2, :], sink[:, kv * G:kv * G + G],
                                        minus_max[:, n % 2, :], ALU.add).then_inc(sink_in, 1)

            def normalise(c, n):
                lo, hi = key_tiles(c, n // 2)
                dve.wait_ge(exp_done, count(c, UNITS, n + 1))
                nc.vector.tensor_tensor(row_sum[:, n % 2, :], row_sum[:, n % 2, :],
                                        sink_term[:, n % 2, :], ALU.add).then_inc(den_done, 1)
                dve.wait_ge(den_done, count(c, 2 * UNITS, 2 * n + 1))
                nc.vector.reciprocal(row_sum[:, n % 2, :], row_sum[:, n % 2, :]).then_inc(den_done, 1)
                dve.wait_ge(den_done, count(c, 2 * UNITS, 2 * n + 2))
                for j in range(2):
                    pj = p[:, n % 2, j, lo * P:hi * P]
                    ins = nc.vector.tensor_scalar(pj, pj, row_sum[:, n % 2, j:j + 1], None, ALU.mult)
                ins.then_inc(norm_done, 1)

            def pt_los(c, n):
                lo, hi = key_tiles(c, n // 2)
                for kt in range(lo, hi):
                    dve.wait_ge(pt_hi_done, count(c, 3 * UNITS, 3 * n + kt + 1))
                    nc.vector.tensor_tensor(pt_lo[kt], t_bank[kt][:, :], pt_hi[kt].bitcast(F32),
                                            ALU.subtract).then_inc(pt_lo_done, signals(lo, hi, kt))

            def output_sum(c, n):
                rows = slice(n % 2 * HD, (n % 2 + 1) * HD)
                dve.wait_ge(low_read, count(c, UNITS, n + 1))
                nc.vector.scalar_tensor_tensor(prod[rows, :, :],
                                               pv_bank[0:HD, :].rearrange("p (j q) -> p j q", j=G), 0.5,
                                               prod[rows, :, :], ALU.mult, ALU.add).then_inc(pv_read, 1)

            def pooled(c, g):
                win = WINDOWS[g]
                total = sums[:, g % 2, :]
                here = u[:, g, LEFT:LEFT + T]
                dve.wait_ge(sum_step, count(c, 10, (g + 1) * (g + 2) // 2))
                lo = win // 2 if is_first(c) else 0
                hi = T - (win // 2 - 1) if is_last(c) else T
                ends = []
                if lo:
                    ends.append((slice(0, lo), recip[:, win // 2 - 1:win - 1]))
                if hi < T:
                    ends.append((slice(hi, T), recip_down[:, 16 - win + 1:16 - win // 2]))
                for cols, r in ends:
                    nc.vector.tensor_tensor(total[:, cols], total[:, cols], r, ALU.mult)\
                      .then_inc(edge_done, 1)
                    edges[0] += 1
                    dve.wait_ge(edge_done, edges[0])
                    nc.vector.tensor_tensor(pooled_at(g)[:, cols], total[:, cols], here[:, cols],
                                            ALU.subtract)
                nc.vector.scalar_tensor_tensor(pooled_at(g)[:, lo:hi], total[:, lo:hi], 1.0 / win,
                                               here[:, lo:hi], ALU.mult, ALU.subtract)\
                  .then_inc(pooled_f, 1)

            edges = [0]

            def gate_mixed(c, g):
                dve.wait_ge(tile_done, count(c, NW, INDEX[("mix", g)] + 1))
                nc.vector.scalar_tensor_tensor(zb[:, g % 2, :], mix_bank[:, :],
                                               half_scale[:, g:g + 1], zb[:, g % 2, :], ALU.mult,
                                               ALU.mult).then_inc(mix_read, 1)

            def merge(c, j):
                dve.wait_ge(tile_done, count(c, NW, INDEX[("ab", j)] + 1))
                dve.wait_ge(*last_read(c, ("gb", j)))
                for a in range(2):
                    gt = gate[:, j % 2, a, :]
                    nc.vector.scalar_tensor_tensor(gt, gt, 1.0, bank[2 * (j % 2) + a][:, :], ALU.add,
                                                   ALU.mult).then_inc(gated, 1)
                dve.wait_ge(gated, count(c, 2 * KD, 2 * j + 2))
                nc.vector.tensor_tensor(gate[:, j % 2, 0, :], gate[:, j % 2, 0, :], gate[:, j % 2, 1, :],
                                        ALU.add).then_inc(merged_f, 1)
                dve.wait_ge(merged_h, count(c, KD, j + 1))
                nc.vector.tensor_tensor(mg_lo[j], gate[:, j % 2, 0, :], mg_hi[j].bitcast(F32),
                                        ALU.subtract).then_inc(merged_l, 1)

            def carry_kvu(c):
                dve.wait_ge(pv_done, count(c, UNITS, UNITS))
                dve.wait_ge(sum_step, count(c, 10, 10))
                for t in (*k_hi, k_lo):
                    nc.vector.tensor_copy(t[:, 0:2 * P], t[:, T:T + 2 * P].bitcast(F32))\
                      .then_inc(kvu_moved, 1)
                nc.vector.tensor_copy(v[:, 0:2, :, :, :], v[:, NB:NB + 2, :, :, :].bitcast(F32))\
                  .then_inc(kvu_moved, 1)
                nc.vector.tensor_copy(u[:, :, 0:FRESH], u[:, :, T:T + FRESH]).then_inc(kvu_moved, 1)

            def v_lo_of(c):
                nt = fresh(c) // P
                dve.wait_ge(v_hi_done, count(c, 1, 1))
                ins = nc.vector.tensor_tensor(
                    v[:, 2:2 + nt, :, 1, :],
                    t_bank[0][:, 0:nt * P].rearrange("p (b v f) -> p b v f", v=2, f=HD),
                    v[:, 2:2 + nt, :, 0, :].bitcast(F32), ALU.subtract)
                if is_first(c):
                    ins = nc.vector.tensor_tensor(
                        v[:, 1, :, 1, :], t_bank[1][:, 0:P].rearrange("p (v f) -> p v f", v=2),
                        v[:, 1, :, 0, :].bitcast(F32), ALU.subtract)
                ins.then_inc(v_lo_done, 1)

            def finish(c, tiles):
                for t in tiles:
                    if t[0] == "ab":
                        merge(c, t[1])
                    elif t[0] not in ("mix", "out"):
                        evacuate(c, t)
                for t in tiles:
                    split(c, INDEX[t] + SPLITS)

            def chunk(c):
                for t in HEAD_TILES[:-1]:
                    finish(c, [t])
                    if t == ("q", 1):
                        v_lo_of(c)
                for s, tiles in enumerate(STEPS):
                    if s == UNITS:
                        finish(c, STEPS[s - 1])
                    if s < UNITS:
                        maxima(c, s)
                    if s:
                        pt_los(c, s - 1)
                    if s < UNITS:
                        finish(c, STEPS[s - 1] if s else HEAD_TILES[-1:])
                    if tiles[0][0] == "mix":
                        gate_mixed(c, tiles[0][1])
                    if s < UNITS:
                        normalise(c, s)
                    if s == UNITS:
                        output_sum(c, s - 1)
                    if s >= 2 and s % 2 == 0:
                        pooled(c, s // 2 - 1)
                    if 0 < s < UNITS:
                        output_sum(c, s - 1)
                finish(c, STEPS[-1])
                gate_mixed(c, NG - 1)
                finish(c, GATE_TILES[:2])
                for t in GATE_TILES[2:]:
                    finish(c, [t])
                    if t == ("ab", 2) and not is_last(c):
                        carry_kvu(c)
                w = INDEX[("out", 0)]
                for i in range(8):
                    if i == 0 and not is_last(c):
                        dve.wait_ge(tile_done, count(c, NW, INDEX[("ab", KD - 1)] + 1))
                        for t in (h_hi, h_lo):
                            nc.vector.tensor_copy(t[:, :, 0:P], t[:, :, T:T + P].bitcast(F32))\
                              .then_inc(h_moved, 1)
                    if i == 3 or i == 7:
                        for m in range(NB):
                            half = slice(0, T) if i == 3 else slice(T, D)
                            if m < NB - 1:
                                dve.wait_ge(out_done, count(c, 2 * (NB - 1), (i // 4) * (NB - 1) + m + 1))
                            else:
                                dve.wait_ge(tile_done, count(c, NW, w + 1))
                            dve.wait_ge(res_in[m], count(c, 1, 1, 16))
                            nc.vector.scalar_tensor_tensor(y[:, m, half], bank[m][:, :], 0.5,
                                                           y[:, m, half], ALU.mult, ALU.add)\
                              .then_inc(y_done, 1)
                    split(c, w + SPLITS)
                    w += 1
                    if not is_last(c):
                        if i in (0, 1):
                            rows_norm(c, NB, AHEAD + i + 1, i % 2)
                        if 2 <= i < 6:
                            rows_lo(c, NB, AHEAD + i - 1, P + (i - 2) * P)
                        if i in (3, 4):
                            rows_norm(c, NB, AHEAD + i, (i - 1) % 2)
                for m in range(NB):
                    dve.wait_ge(y_rstd, count(c, NB, m + 1))
                    nc.vector.scalar_tensor_tensor(y[:, m, :], y[:, m, :], rstd[:, m:m + 1],
                                                   g_final[:, :], ALU.mult, ALU.mult).then_inc(y_norm, 1)

            over_chunks(dve, chunk)

        @block.tensor
        def _(pe):
            def passes(dst, a, b, start, stop):
                nc.tensor.matmul(dst, a[0], b[0], start=start, stop=False)
                nc.tensor.matmul(dst, a[0], b[1], start=False, stop=False)
                return nc.tensor.matmul(dst, a[1], b[0], start=False, stop=stop)

            def w_at(w, k):
                cols = slice(k * P, (k + 1) * P)
                return w_hi[:, w % SPLITS, cols], w_lo[:, w % SPLITS, cols]

            def h_at(k, lo, n):
                return h_hi[:, k, lo:lo + n], h_lo[:, k, lo:lo + n]

            def turn_rows(c, per, i, slot, b=4):
                pe.wait_ge(x_norm, count(c, per, i))
                if per or i > 4:
                    pe.wait_ge(h_lo_done, count(c, per, i - (1 if per else 4)))
                for k in range(KD):
                    ins = nc.tensor.transpose(bank[b + k // 4][:, (k % 4) * P:(k % 4 + 1) * P],
                                              xn[:, slot, k * P:(k + 1) * P], ident[:, :])
                ins.then_inc(x_turned, 1)

            def dense(c, t, ks=range(KD)):
                kind, j = t
                w = INDEX[t]
                ahead = kind in ("k", "v", "u")
                n = fresh(c) if ahead else T
                at = P if ahead else 0
                dst = dense_bank(t)
                if ks[0] == 0:
                    i = DENSE.index(t)
                    pe.wait_ge(split_lo, count(c, NW, w + 1))
                    pe.wait_ge(*last_read(c, DENSE[i - 2], back=1 if i < 2 else 0))
                for k in ks:
                    ins = passes(dst[:, 0:n], w_at(w, k), h_at(k, at, n), k == 0, k == KD - 1)
                if ks[-1] == KD - 1:
                    if is_first(c) and ahead:
                        dst = {"k": bank[0], "v": bank[1], "u": u_bank}[kind]
                        if kind == "u":
                            pe.wait_ge(pt_lo_done, count(c, 3 * UNITS, 6 * j))
                        for k in range(KD):
                            ins = passes(dst[:, 0:P], w_at(w, k), h_at(k, 0, P), k == 0, k == KD - 1)
                    ins.then_inc(tile_done, 1)

            def turn_v(c):
                pe.wait_ge(*last_read(c, ("v", 0)))
                pe.wait_ge(y_done, count(c, 8, 0))
                for b in range(fresh(c) // P):
                    ins = nc.tensor.transpose(t_bank[0][:, b * P:(b + 1) * P], v_t[:, b * P:(b + 1) * P],
                                              ident[:, :])
                if is_first(c):
                    ins = nc.tensor.transpose(t_bank[1][:, 0:P], v_t[:, T:T + P], ident[:, :])
                ins.then_inc(v_turned, 1)

            def scores(c, n, heads):
                b, kv = divmod(n, 2)
                lo, hi = key_tiles(c, b)
                rows = slice(kv * HD, (kv + 1) * HD)
                keys = slice((b + lo) * P, (b + hi) * P)
                if n == 0:
                    pe.wait_ge(*last_read(c, ("q", 3)))
                for j in heads:
                    if j == 1 and n >= 4 and n % 2 == 0:
                        pe.wait_ge(mix_read, count(c, NG, (n - 2) // 2))
                    pe.wait_ge(max_done, count(c, 4 * UNITS, 4 * n + j - 1))
                    queries = slice(b * P, (b + 1) * P)
                    dst = bank[j % 2][:, lo * P:hi * P]
                    nc.tensor.matmul(dst, qa[kv][:, j, queries], k_hi[kv][:, keys], start=True,
                                     stop=False)
                    nc.tensor.matmul(dst, qa[kv][rows, j, queries], k_lo[rows, keys], start=False,
                                     stop=True).then_inc(qk_done, 1)

            def turn_p(c, n):
                lo, hi = key_tiles(c, n // 2)
                pe.wait_ge(norm_done, count(c, UNITS, n + 1))
                pe.wait_ge(norm_act, count(c, UNITS, n + 1))
                for kt in range(lo, hi):
                    pe.wait_ge(pt_lo_done, count(c, 3 * UNITS, 3 * (n - 1) + kt + 1))
                    if is_first(c) and kt == 2:
                        pe.wait_ge(*last_read(c, ("u", n // 2)))
                    for j in range(G):
                        ins = nc.tensor.transpose(t_bank[kt][:, j * P:(j + 1) * P],
                                                  p[:, n % 2, j, kt * P:(kt + 1) * P], ident[:, :])
                    ins.then_inc(pt_done, signals(lo, hi, kt))

            def values(c, n):
                b, kv = divmod(n, 2)
                lo, hi = key_tiles(c, b)
                pe.wait_ge(pv_read, count(c, UNITS, n))
                if n == 0:
                    pe.wait_ge(v_lo_done, count(c, 1, 1))
                for kt in range(lo, hi):
                    pe.wait_ge(pt_lo_done, count(c, 3 * UNITS, 3 * n + kt + 1))
                    v_block = v[:, b + kt, kv, :, :]
                    nc.tensor.matmul(pv_bank[:, :], v_block, pt_hi[kt], start=kt == lo, stop=False)
                    ins = nc.tensor.matmul(pv_bank[:, :], v_block, pt_lo[kt], start=False,
                                           stop=kt == hi - 1)
                ins.then_inc(pv_done, 1)

            def mix(c, g):
                w = INDEX[("mix", g)]
                pe.wait_ge(split_lo, count(c, NW, w + 1))
                pe.wait_ge(max_done, count(c, 4 * UNITS, 4 * min(2 * g + 4, UNITS)))
                pe.wait_ge(pooled_l, count(c, NG, g + 1))
                passes(mix_bank[:, :], w_at(w, 0), (pooled_hi, pooled_lo), True,
                       True).then_inc(tile_done, 1)

            def branches(c, j):
                w = INDEX[("ab", j)]
                pe.wait_ge(split_lo, count(c, NW, w + 1))
                if j:
                    pe.wait_ge(gated, count(c, 2 * KD, 2 * (j - 1)))
                for a, (hi, lo) in enumerate((qa, (po_hi, po_lo))):
                    if j == 0 and a == 0:
                        pe.wait_ge(at_lo_done, count(c, NB, NB))
                    if j == 0 and a == 1:
                        pe.wait_ge(po_lo_done, count(c, NG, NG))
                    for k in range(4):
                        ins = passes(bank[2 * (j % 2) + a][:, :], w_at(w, 4 * a + k),
                                     (hi[:, k, :], lo[:, k, :]), k == 0, k == 3)
                ins.then_inc(tile_done, 1)

            def output(c, i):
                w = INDEX[("out", i)]
                half, pair = divmod(i, 4)
                pe.wait_ge(split_lo, count(c, NW, w + 1))
                if half == 0:
                    pe.wait_ge(merged_l, count(c, KD, 2 * pair + 2))
                for m in range(NB):
                    if i == 0 and m == 2:
                        pe.wait_ge(gated, count(c, 2 * KD, 2 * KD))
                    if pair == 0 and half == 1:
                        pe.wait_ge(y_done, count(c, 8, m + 1))
                    for e in range(2):
                        k = 2 * pair + e
                        tok = slice(m * P, (m + 1) * P)
                        rhs = (w_hi[:, w % SPLITS, e * T:(e + 1) * T],
                               w_lo[:, w % SPLITS, e * T:(e + 1) * T])
                        ins = passes(bank[m][:, :], (mg_hi[k][:, tok], mg_lo[k][:, tok]), rhs,
                                     k == 0, k == KD - 1)
                    if pair == 3 and m < NB - 1:
                        ins.then_inc(out_done, 1)
                ins.then_inc(tile_done, 1)

            pe.wait_ge(s_made, 5)
            for i in range(AHEAD):
                turn_rows(0, 0, i + 1, i, 2 * (i % 4))

            def chunk(c):
                if is_first(c):
                    pe.wait_ge(h_lo_done, AHEAD)
                else:
                    pe.wait_ge(h_lo_done, count(c, NB, AHEAD))
                for t in HEAD_TILES:
                    dense(c, t)
                    if t == ("q", 1):
                        turn_v(c)
                for s, tiles in enumerate(STEPS):
                    before = 2 if s < UNITS else 4
                    after = 7 if s < UNITS else KD
                    if s < UNITS:
                        scores(c, s, range(0, 2))
                    dense(c, tiles[-1], range(0, before))
                    if s < UNITS:
                        scores(c, s, range(2, G))
                    if s:
                        turn_p(c, s - 1)
                    dense(c, tiles[-1], range(before, after))
                    if len(tiles) > 1:
                        mix(c, tiles[0][1])
                    if s:
                        values(c, s - 1)
                    if after < KD:
                        dense(c, tiles[-1], range(after, KD))
                for t in GATE_TILES:
                    if t[0] == "ab":
                        branches(c, t[1])
                    elif t[0] == "mix":
                        mix(c, t[1])
                    else:
                        dense(c, t)
                for i in range(8):
                    output(c, i)
                    if 2 <= i < 6 and not is_last(c):
                        turn_rows(c, NB, AHEAD + i - 1, (i - 2) % 2)

            over_chunks(pe, chunk)


def kernel(x, norm_g, w_in, attn_sink, pool_w, pool_scale, w_branch_a, w_branch_b, w_out, final_norm_g):
    import numpy as np
    import concourse.bacc as bacc
    from concourse.bass_utils import run_bass_kernel_spmd

    def lay(a):
        return np.ascontiguousarray(a)

    heads = np.arange(NH * HD).reshape(2, G, HD).transpose(1, 0, 2).ravel()
    w = np.asarray(w_in)[0]
    off = np.cumsum([0, 512, 128, 128, 512, 512, 512, 1024, 1024])
    cols = np.concatenate([heads, np.arange(off[1], off[3]), off[3] + heads, np.arange(off[4], off[8])])
    w_in_t = lay(w[:, cols].reshape(KD, P, -1, P).transpose(2, 1, 0, 3).reshape(-1, P, D))
    ab = np.concatenate([np.asarray(w_branch_a)[0][heads], np.asarray(w_branch_b)[0]])
    w_ab_t = lay(ab.reshape(8, P, KD, P).transpose(2, 1, 0, 3).reshape(KD, P, D))
    w_out_t = lay(np.asarray(w_out)[0].reshape(4, 2, P, 2, T).transpose(3, 0, 2, 1, 4).reshape(8, P, D))
    arrays = {
        "in_x": lay(np.asarray(x)[0]), "in_w_in": w_in_t, "in_w_ab": w_ab_t, "in_w_out": w_out_t,
        "in_pool_w": lay(np.asarray(pool_w)[0]), "in_sink": lay(np.asarray(attn_sink)),
        "in_pool_scale": lay(np.asarray(pool_scale).reshape(NG, P)), "in_norm_g": lay(np.asarray(norm_g)),
        "in_final_g": lay(np.asarray(final_norm_g).reshape(1, D)),
    }
    nc = bacc.Bacc("TRN2", target_bir_lowering=False, num_devices=1)
    ap = {k: nc.dram_tensor(k, a.shape, mybir.dt.from_np(a.dtype), kind="ExternalInput").ap()
          for k, a in arrays.items()}
    out = nc.dram_tensor("out", (S, D), F32, kind="ExternalOutput").ap()
    build(nc, ap["in_x"], ap["in_w_in"], ap["in_w_ab"], ap["in_w_out"], ap["in_pool_w"], ap["in_sink"],
          ap["in_pool_scale"], ap["in_norm_g"], ap["in_final_g"], out)
    r = run_bass_kernel_spmd(nc, [arrays], core_ids=[0])
    return r.results[0]["out"].reshape(1, S, D)
```

```python
from contextlib import ExitStack

import concourse.bass as bass
from concourse import mybir

F32 = mybir.dt.float32
F32R = mybir.dt.float32r
BF16 = mybir.dt.bfloat16
ALU = mybir.AluOpType
ACT = mybir.ActivationFunctionType

P = 128
D = 1024
S = 4096
HD = 64
NH = 8
G = 4
WINDOWS = (2, 4, 8, 16)
NG = len(WINDOWS)
EPS = 1e-6
MASKED = -1e30
T = 512
NB = T // P
CHUNKS = S // T
LAST = CHUNKS - 1
KD = D // P
HW = T + P
KW = T + 2 * P
LEFT = 8
UW = LEFT + HW
FRESH = LEFT + P
UNITS = 2 * NB

HEAD_TILES = [("k", 0), ("v", 0)] + [("q", j) for j in range(4)] + [("za", j) for j in range(4)]
STEPS = [[("u", 0)], [("zb", 0)], [("u", 1)], [("mix", 0), ("zb", 1)], [("u", 2)],
         [("mix", 1), ("zb", 2)], [("u", 3)], [("mix", 2), ("zb", 3)], [("ga", 0)]]
GATE_TILES = [("gb", 0), ("mix", 3), ("ga", 1), ("ab", 0), ("gb", 1), ("ab", 1)] +\
             [(k, j) for j in range(2, KD) for k in ("ga", "gb", "ab")]
OUT_TILES = [("out", i) for i in range(8)]
TILES = HEAD_TILES + [t for s in STEPS for t in s] + GATE_TILES + OUT_TILES
INDEX = {t: w for w, t in enumerate(TILES)}
NW = len(TILES)
SPLITS = 3
RAWS = 3
XTS = 4
H_TILES = [[], [], [0], [1, 2], [3], [4, 5], [6, 7], []]
X_T_BEHIND = [[], [], [], [0], [1, 2], [3], [4], [5, 6, 7]]
RESIDUAL_AT = [INDEX[("ga", 2)] + 2 * m for m in range(NB)]
EARLY = 2
DENSE = [t for t in TILES if t[0] not in ("mix", "ab", "out")]
DVE_LAST = [t for t in DENSE if t[0] in ("k", "q", "za", "zb")]
ACT_LAST = [t for t in DENSE if t[0] in ("v", "u", "ga", "gb")]
assert NW % SPLITS == 0 and NW % RAWS == 0 and len(DENSE) % 2 == 0


def cols_of(kind):
    return P if kind == "mix" else D


def build(nc, x, x_t, w_in_t, w_ab_t, w_out_t, pool_w, attn_sink, pool_scale, norm_g, norm_g_t,
          final_g, out):
    with ExitStack() as ctx:
        def sb(name, shape, dt=F32):
            return ctx.enter_context(nc.sbuf_tensor(name, shape, dt))

        def sem(name):
            return ctx.enter_context(nc.semaphore(name))

        h_hi = sb("h_hi", [P, KD, HW], F32R)
        h_lo = sb("h_lo", [P, KD, HW], F32R)
        qa = [sb(f"qa{kv}", [P, 4, T], F32R) for kv in range(2)]
        po_hi = sb("po_hi", [P, NG, T], F32R)
        po_lo = sb("po_lo", [P, NG, T], F32R)
        arena_r = sb("arena_r", [P, 8 * 2 * T], F32R)
        arena_f = sb("arena_f", [P, 6 * D])
        k_hi = [sb(f"k_hi{kv}", [P, KW], F32R) for kv in range(2)]
        k_lo = sb("k_lo", [P, KW], F32R)
        v = sb("v", [P, KW // P, 2, 2, HD], F32R)
        u = sb("u", [P, NG, UW])
        sums = sb("sums", [P, 2, T + 16])
        raw = sb("raw", [P, RAWS, D])
        g_norm = raw[:, RAWS - 1, :]
        w_hi = sb("w_hi", [P, SPLITS, D], F32R)
        w_lo = sb("w_lo", [P, SPLITS, D], F32R)
        bias = sb("bias", [P, NH, 3 * P], BF16)
        g_col = sb("g_col", [P, KD])
        g_final = sb("g_final", [P, D])
        ident = sb("ident", [P, P])
        eps = sb("eps", [P, 1])
        minus_half = sb("minus_half", [P, 1])
        recip = sb("recip", [P, 16])
        recip_down = sb("recip_down", [P, 16])
        sink = sb("sink", [P, NH])
        minus_sink = sb("minus_sink", [P, NH])
        half_scale = sb("half_scale", [P, NG])
        row_max = sb("row_max", [P, 2, G])
        minus_max = sb("minus_max", [P, 2, G])
        row_sum = sb("row_sum", [P, 2, G])
        sink_term = sb("sink_term", [P, 2, G])
        waiter = sb("waiter", [P, 2, G])
        ssq = sb("ssq", [P, 9])
        ms = sb("ms", [P, 9])
        rstd = sb("rstd", [P, 9])

        v_t = arena_f[:, 0:HW]
        p = arena_f[:, 0:2 * G * 3 * P].rearrange("p (b h k) -> p b h k", b=2, h=G)
        za = arena_f[:, 3 * D:5 * D].rearrange("p (j t) -> p j t", j=4)
        zb = arena_f[:, 5 * D:6 * D].rearrange("p (j t) -> p j t", j=2)
        gate = arena_f[:, 0:2 * D].rearrange("p (b a t) -> p b a t", b=2, a=2)
        xn = arena_f[:, :].rearrange("p (b f) -> p b f", b=6)
        xt = arena_f[:, 0:2 * D].rearrange("p (b t) -> p b t", b=XTS)
        y = arena_f[:, 2 * D:6 * D].rearrange("p (m f) -> p m f", m=NB)
        prod = sb("prod", [P, G, P])
        row = sums[:, :, :].rearrange("p a b -> p (a b)")[:, 0:D]
        rstd_wide = prod
        junk = sums[:, :, :].rearrange("p a b -> p (a b)").bitcast(BF16)[:, 0:D]
        pt_hi = [arena_r[:, kt * 2 * T:kt * 2 * T + T] for kt in range(3)]
        pt_lo = [arena_r[:, kt * 2 * T + T:(kt + 1) * 2 * T] for kt in range(3)]
        pooled_hi = arena_r[:, 6 * T:7 * T]
        pooled_lo = arena_r[:, 7 * T:8 * T]
        mg_hi = [arena_r[:, j * 2 * T:j * 2 * T + T] for j in range(KD)]
        mg_lo = [arena_r[:, j * 2 * T + T:(j + 1) * 2 * T] for j in range(KD)]

        bank = [ctx.enter_context(nc.psum_tensor(f"bank{i}", [P, T], F32)) for i in range(8)]
        mix_bank, pv_bank, t_bank = bank[1], bank[2], bank[3:6]
        u_bank = t_bank[2]
        rstd_bank = bank[4]

        gain_in = sem("gain_in")
        s_const = sem("s_const")
        s_made = sem("s_made")
        s_abs = sem("s_abs")
        s_cdve = sem("s_cdve")
        raw_in = [sem(f"raw_in{i}") for i in range(RAWS)]
        split_hi = sem("split_hi")
        split_lo = sem("split_lo")
        tile_done = sem("tile_done")
        act_read = sem("act_read")
        dve_read = sem("dve_read")
        hi_kq = sem("hi_kq")
        mix_read = sem("mix_read")
        tanh_z = sem("tanh_z")
        v_turned = sem("v_turned")
        v_hi_done = sem("v_hi_done")
        v_lo_done = sem("v_lo_done")
        qk_done = sem("qk_done")
        max_done = sem("max_done")
        neg_done = sem("neg_done")
        sink_in = sem("sink_in")
        exp_done = sem("exp_done")
        den_done = sem("den_done")
        norm_done = sem("norm_done")
        norm_act = sem("norm_act")
        pt_done = sem("pt_done")
        pt_hi_done = sem("pt_hi_done")
        pt_lo_done = sem("pt_lo_done")
        pv_done = sem("pv_done")
        low_read = sem("low_read")
        pv_read = sem("pv_read")
        prod_done = sem("prod_done")
        at_hi_done = sem("at_hi_done")
        at_lo_done = sem("at_lo_done")
        sum_step = sem("sum_step")
        pooled_f = sem("pooled_f")
        edge_done = sem("edge_done")
        pooled_h = sem("pooled_h")
        pooled_l = sem("pooled_l")
        po_hi_done = sem("po_hi_done")
        po_lo_done = sem("po_lo_done")
        gated = sem("gated")
        merged_f = sem("merged_f")
        merged_h = sem("merged_h")
        merged_l = sem("merged_l")
        kvu_moved = sem("kvu_moved")
        h_moved = sem("h_moved")
        x_first = [sem(f"x_first{i}") for i in range(NB + 1)]
        x_in = sem("x_in")
        xt_in = [sem(f"xt_in{i}") for i in range(XTS)]
        x_sq = sem("x_sq")
        x_ms = sem("x_ms")
        x_rstd = sem("x_rstd")
        x_norm = sem("x_norm")
        x_turned = sem("x_turned")
        rstd_made = sem("rstd_made")
        rstd_turned = sem("rstd_turned")
        xt_scaled = sem("xt_scaled")
        h_hi_done = sem("h_hi_done")
        h_lo_done = sem("h_lo_done")
        res_in = [sem(f"res_in{m}") for m in range(NB)]
        out_done = sem("out_done")
        y_done = sem("y_done")
        y_sq = sem("y_sq")
        y_ms = sem("y_ms")
        y_rstd = sem("y_rstd")
        y_norm = sem("y_norm")
        stored = [sem(f"stored{m}") for m in range(NB)]

        N_CONST = 4
        AHEAD = NB + 1

        def count(c, per, i, unit=1):
            value = (c * per + i) * unit
            return max(value, 0) if isinstance(c, int) else value

        def last_read(c, t, back=0):
            if t in DVE_LAST:
                return dve_read, count(c, len(DVE_LAST), DVE_LAST.index(t) + 1 - back * len(DVE_LAST))
            return act_read, count(c, len(ACT_LAST), ACT_LAST.index(t) + 1 - back * len(ACT_LAST))

        def dense_bank(t):
            return bank[6 + DENSE.index(t) % 2]

        def fresh(c):
            return T - P if is_last(c) else T

        def is_first(c):
            return isinstance(c, int) and c == 0

        def is_last(c):
            return isinstance(c, int) and c == LAST

        def key_tiles(c, b):
            lo = 1 if is_first(c) and b == 0 else 0
            hi = 2 if is_last(c) and b == NB - 1 else 3
            return lo, hi

        def over_chunks(eng, chunk):
            chunk(0)
            with eng.Fori(1, LAST) as c:
                chunk(c)
            chunk(LAST)

        def signals(lo, hi, kt):
            return 2 if (lo == 1 and kt == 1) or (hi == 2 and kt == 1) else 1

        def pooled_at(g):
            return sums[:, 1 - g % 2, 0:T]

        block = ctx.enter_context(nc.Block())

        @block.sync
        def _(sp):
            def load_weight(c, w):
                kind, j = TILES[w]
                n = cols_of(kind)
                at = {"q": 0, "k": 4, "v": 5, "za": 6, "u": 10, "zb": 14, "ga": 18, "gb": 26}
                src = (pool_w[j] if kind == "mix" else w_ab_t[j] if kind == "ab" else
                       w_out_t[j] if kind == "out" else w_in_t[at[kind] + j])
                sp.wait_ge(split_lo, count(c, NW, w + 1 - RAWS))
                sp.dma_start(raw[:, w % RAWS, 0:n], src).then_inc(raw_in[w % RAWS], 16)

            def load_rows(c, m):
                if m == 0:
                    sp.wait_ge(pooled_l, count(c, NG, NG))
                else:
                    sp.wait_ge(x_sq, count(c, NB, AHEAD + m))
                tile = (c * NB + AHEAD + m) % (S // P)
                sp.dma_start(row, x[bass.ds(tile * P, P), :]).then_inc(x_in, 16)

            def load_x_t(c, k):
                if k < XTS:
                    sp.wait_ge(merged_l, count(c, KD, KD))
                else:
                    sp.wait_ge(h_lo_done, count(c, KD, AHEAD + k - XTS + 1))
                sp.dma_start(xt[:, k % XTS, :], x_t[k, :, bass.ds(c * T + T + P, T)])\
                  .then_inc(xt_in[k % XTS], 16)

            def chunk(c):
                for w in range(NW):
                    if w == INDEX[("ga", 2)]:
                        sp.wait_ge(pt_done, count(c, 3 * UNITS, 3 * UNITS))
                        sp.wait_ge(prod_done, count(c, NB, NB))
                        sp.wait_ge(po_lo_done, count(c, NG, NG))
                    if w in RESIDUAL_AT:
                        m = RESIDUAL_AT.index(w)
                        sp.dma_start(y[:, m, :], x[bass.ds(c * T + m * P, P), :]).then_inc(res_in[m], 16)
                    if not is_last(c):
                        if TILES[w][0] == "gb" and 4 <= TILES[w][1] < 4 + NB:
                            load_rows(c, TILES[w][1] - 4)
                    if is_first(c) and w == RAWS - 1:
                        sp.wait_ge(x_norm, AHEAD)
                    if not (is_first(c) and w < EARLY):
                        load_weight(c, w)
                    if TILES[w][0] == "out" and not is_last(c):
                        for k in X_T_BEHIND[TILES[w][1]]:
                            load_x_t(c, k)

            for i in range(AHEAD):
                sp.dma_start(xn[:, i, :], x[i * P:(i + 1) * P, :]).then_inc(x_first[i], 16)
                if i == 1:
                    load_weight(0, 0)
            load_weight(0, 1)
            over_chunks(sp, chunk)
            for m in range(NB):
                sp.wait_ge(stored[m], 16 * CHUNKS)

        @block.gpsimd
        def _(pool):
            nc.gpsimd.memset(ident[:, :], 0.0).then_inc(s_made, 1)
            nc.gpsimd.memset(eps[:, :], EPS).then_inc(s_made, 1)
            nc.gpsimd.memset(minus_half[:, :], -0.5).then_inc(s_made, 1)
            nc.gpsimd.memset(u[:, :, 0:LEFT], 0.0).then_inc(s_made, 1)
            pool.wait_ge(s_made, 4)
            nc.gpsimd.affine_select(out=ident[:, :], in_=ident[:, :], compare_op=ALU.not_equal, fill=1.0,
                                    base=0, pattern=[[-1, P]], channel_multiplier=1).then_inc(s_made, 1)

            def rstd_of(c, per, i, col, sq, ms_sem, rs_sem):
                pool.wait_ge(sq, count(c, per, i))
                nc.gpsimd.tensor_tensor(ms[:, col:col + 1], ssq[:, col:col + 1], eps[:, :],
                                        ALU.add).then_inc(ms_sem, 1)
                pool.wait_ge(ms_sem, count(c, per, i))
                nc.gpsimd.tensor_tensor(rstd[:, col:col + 1], ms[:, col:col + 1], minus_half[:, :],
                                        ALU.pow).then_inc(rs_sem, 1)

            for i in range(2):
                rstd_of(0, 0, i + 1, 4 + i, x_sq, x_ms, x_rstd)
            dist = arena_f[:, 5 * D:5 * D + 3 * P]
            nc.gpsimd.iota(dist, pattern=[[-1, 3 * P]], base=P, channel_multiplier=1,
                           allow_small_or_imprecise_dtypes=True).then_inc(s_made, 1)
            nc.gpsimd.iota(recip[:, :], pattern=[[1, 16]], base=1, channel_multiplier=0,
                           allow_small_or_imprecise_dtypes=True).then_inc(s_made, 1)
            nc.gpsimd.iota(recip_down[:, :], pattern=[[-1, 16]], base=16, channel_multiplier=0,
                           allow_small_or_imprecise_dtypes=True).then_inc(s_made, 1)
            for i in range(2, AHEAD):
                rstd_of(0, 0, i + 1, 4 + i, x_sq, x_ms, x_rstd)
            pool.wait_ge(s_cdve, 8)
            nc.gpsimd.affine_select(out=bias[:, :, :], in_=bias[:, :, :], compare_op=ALU.is_ge, fill=MASKED,
                                    base=0, pattern=[[0, NH], [1, 3 * P]], channel_multiplier=-1)\
                     .then_inc(s_made, 1)
            pool.wait_ge(s_made, 9)
            nc.gpsimd.affine_select(out=bias[:, :, :], in_=bias[:, :, :], compare_op=ALU.is_ge, fill=MASKED,
                                    base=2 * P, pattern=[[0, NH], [-1, 3 * P]], channel_multiplier=1)\
                     .then_inc(s_made, 1)

            def window_sums(c, g):
                win = WINDOWS[g]
                a = LEFT - win // 2
                step, width, src = 1, T + win - 2, u[:, g, a:a + T + win - 1]
                pool.wait_ge(*last_read(c, ("u", g)))
                if g:
                    pool.wait_ge(pooled_l, count(c, NG, g))
                else:
                    pool.wait_ge(y_sq, count(c, NB, 0))
                    pool.wait_ge(pooled_l, count(c, NG, 0))
                which, done = 0, g * (g + 1) // 2
                while True:
                    dst = sums[:, which, 0:width]
                    if step > 1:
                        pool.wait_ge(sum_step, count(c, 10, done))
                    nc.gpsimd.tensor_tensor(dst, src[:, 0:width], src[:, step:step + width],
                                            ALU.add).then_inc(sum_step, 1)
                    done += 1
                    step *= 2
                    if step == win:
                        break
                    src, which, width = sums[:, which, :], 1 - which, width - step

            def gate_output(c, b):
                pool.wait_ge(pv_read, count(c, UNITS, 2 * b + 2))
                nc.gpsimd.tensor_tensor(prod[:, :, :], prod[:, :, :], za[:, :, b * P:(b + 1) * P],
                                        ALU.mult).then_inc(prod_done, 1)

            def attention_lo(c, b):
                pool.wait_ge(at_hi_done, count(c, NB, b + 1))
                nc.gpsimd.tensor_tensor(qa[1][:, :, b * P:(b + 1) * P], prod[:, :, :],
                                        qa[0][:, :, b * P:(b + 1) * P].bitcast(F32),
                                        ALU.subtract).then_inc(at_lo_done, 1)

            def pooled_lo_of(c, g):
                pool.wait_ge(pooled_h, count(c, NG, g + 1))
                nc.gpsimd.tensor_tensor(pooled_lo, pooled_at(g), pooled_hi.bitcast(F32),
                                        ALU.subtract).then_inc(pooled_l, 1)

            def pool_out_lo(c, g):
                pool.wait_ge(po_hi_done, count(c, NG, g + 1))
                nc.gpsimd.tensor_tensor(po_lo[:, g, :], zb[:, g % 2, :], po_hi[:, g, :].bitcast(F32),
                                        ALU.subtract).then_inc(po_lo_done, 1)

            def chunk(c):
                if is_last(c):
                    pool.wait_ge(kvu_moved, 5 * LAST)
                    end = LEFT + T
                    nc.gpsimd.memset(u[:, :, end:end + LEFT], 0.0).then_inc(s_made, 1)
                    pool.wait_ge(s_made, 11)
                for s in range(1, len(STEPS)):
                    if s >= 3 and s % 2 == 1:
                        attention_lo(c, (s - 3) // 2)
                    if s % 2 == 1 and s // 2 < NG:
                        window_sums(c, s // 2)
                    if s >= 4 and s % 2 == 0:
                        pool_out_lo(c, (s - 4) // 2)
                    if s % 2 == 0:
                        gate_output(c, s // 2 - 1)
                        pooled_lo_of(c, s // 2 - 1)
                attention_lo(c, NB - 1)
                pool_out_lo(c, NG - 1)
                if not is_last(c):
                    for m in range(NB):
                        rstd_of(c, NB, AHEAD + m + 1, 4 + m, x_sq, x_ms, x_rstd)
                for m in range(NB):
                    rstd_of(c, NB, m + 1, m, y_sq, y_ms, y_rstd)

            over_chunks(pool, chunk)

        @block.scalar
        def _(act):
            def split(c, w):
                if w >= NW and is_last(c):
                    return
                n = cols_of(TILES[w % NW][0])
                act.wait_ge(raw_in[w % RAWS], count(c, NW // RAWS, w // RAWS + 1, 16))
                act.wait_ge(tile_done, count(c, NW, w - SPLITS + 1))
                nc.scalar.activation(w_hi[:, w % SPLITS, 0:n], raw[:, w % RAWS, 0:n],
                                     ACT.Copy).then_inc(split_hi, 1)

            def first_square(i):
                act.wait_ge(x_first[i], 16)
                act.wait_ge(x_sq, i)
                nc.scalar.activation(junk, xn[:, i, :], ACT.Square, scale=D ** -0.5,
                                     accum_out=ssq[:, 4 + i:5 + i]).then_inc(x_sq, 1)

            def rows_square(c, m):
                act.wait_ge(x_in, count(c, NB, m + 1, 16))
                act.wait_ge(x_ms, count(c, NB, AHEAD + m + 1 - NB))
                nc.scalar.activation(row, row, ACT.Square, scale=D ** -0.5,
                                     accum_out=ssq[:, 4 + m:5 + m]).then_inc(x_sq, 1)

            def h_hi_of(c, k):
                if k == 0:
                    act.wait_ge(h_moved, count(c, 2, 2))
                act.wait_ge(xt_scaled, count(c, KD, k + 1))
                nc.scalar.activation(h_hi[:, k, P:P + T], xt[:, k % XTS, :], ACT.Copy).then_inc(h_hi_done, 1)

            def rows_hi(i, at, b):
                act.wait_ge(x_turned, i)
                for half in range(2):
                    ins = nc.scalar.activation(
                        h_hi[:, 4 * half:4 * half + 4, at:at + P],
                        bank[b + half][:, :].rearrange("p (k t) -> p k t", k=4), ACT.Copy)
                ins.then_inc(h_hi_done, 1)

            act.dma_start(g_norm, norm_g.to_broadcast([P, D])).then_inc(gain_in, 16)
            act.dma_start(sink[:, :], attn_sink.to_broadcast([P, NH])).then_inc(s_const, 16)
            with nc.allow_non_contiguous_dma("512 values, once"):
                act.dma_start(half_scale[:, :], pool_scale.rearrange("g p -> p g")).then_inc(s_const, 16)
            for i in range(AHEAD + 2):
                if i < AHEAD:
                    first_square(i)
                if i >= 2:
                    rows_hi(i - 1, (i - 2) * P, 2 + 2 * ((i - 2) % 3))
                if i == 2:
                    split(0, 0)
                    act.dma_start(g_col[:, :], norm_g_t).then_inc(s_const, 16)
                    act.dma_start(g_final[:, :], final_g.to_broadcast([P, D])).then_inc(s_const, 16)
                    act.wait_ge(s_made, 6)
                    dist = arena_f[:, 5 * D:5 * D + 3 * P]
                    nc.scalar.activation(dist, dist, ACT.Abs).then_inc(s_abs, 1)
            for w in range(1, SPLITS):
                split(0, w)

            def evacuate(c, t):
                kind, j = t
                src = dense_bank(t)
                act.wait_ge(tile_done, count(c, NW, INDEX[t] + 1))
                n = fresh(c)
                if kind == "k":
                    act.wait_ge(kvu_moved, count(c, 5, 0))
                    for kv in range(2):
                        rows = slice(kv * HD, (kv + 1) * HD)
                        for to in (slice(0, HD), slice(HD, P)):
                            ins = nc.scalar.activation(k_hi[kv][to, 2 * P:2 * P + n], src[rows, 0:n],
                                                       ACT.Copy)
                            if is_first(c):
                                ins = nc.scalar.activation(k_hi[kv][to, P:2 * P], bank[0][rows, 0:P],
                                                           ACT.Copy)
                    ins.then_inc(hi_kq, 1)
                elif kind == "v":
                    ins = nc.scalar.activation(v_t[:, 0:n], src[:, 0:n], ACT.Copy)
                    if is_first(c):
                        ins = nc.scalar.activation(v_t[:, T:T + P], bank[1][:, 0:P], ACT.Copy)
                    ins.then_inc(act_read, 1)
                elif kind == "q":
                    act.wait_ge(tile_done, count(c, NW, INDEX[("ab", KD - 1)] + 1 - NW))
                    for kv in range(2):
                        rows = slice(kv * HD, (kv + 1) * HD)
                        ins = nc.scalar.activation(qa[kv][rows, j, :], src[rows, :], ACT.Copy,
                                                   scale=HD ** -0.5)
                    ins.then_inc(hi_kq, 1)
                elif kind == "za":
                    if j == 0:
                        for m in range(NB):
                            act.wait_ge(stored[m], count(c, 1, 0, 16))
                    nc.scalar.activation(za[:, j, :], src[:, :], ACT.Tanh, scale=0.5).then_inc(tanh_z, 1)
                elif kind == "zb":
                    if j >= 2:
                        act.wait_ge(po_lo_done, count(c, NG, j - 1))
                    nc.scalar.activation(zb[:, j % 2, :], src[:, :], ACT.Tanh, scale=0.5)\
                      .then_inc(tanh_z, 1)
                elif kind == "u":
                    act.wait_ge(kvu_moved, count(c, 5, 0))
                    ins = nc.scalar.activation(u[:, j, FRESH:FRESH + n], src[:, 0:n], ACT.Copy)
                    if is_first(c):
                        ins = nc.scalar.activation(u[:, j, LEFT:FRESH], u_bank[:, 0:P], ACT.Copy)
                    ins.then_inc(act_read, 1)
                elif kind in ("ga", "gb"):
                    if j < 2:
                        act.wait_ge(pt_done, count(c, 3 * UNITS, 3 * UNITS))
                    else:
                        act.wait_ge(merged_l, count(c, KD, j - 1))
                    nc.scalar.activation(gate[:, j % 2, "ab".index(kind[1]), :], src[:, :], ACT.Tanh,
                                         scale=0.5).then_inc(act_read, 1)

            def exps(c, n):
                b, kv = divmod(n, 2)
                lo, hi = key_tiles(c, b)
                act.wait_ge(neg_done, count(c, UNITS, n + 1))
                for j in range(G):
                    pj = p[:, n % 2, j, lo * P:hi * P]
                    nc.scalar.activation(pj, pj, ACT.Exp, bias=minus_max[:, n % 2, j:j + 1],
                                         accum_out=row_sum[:, n % 2, j:j + 1])
                act.wait_ge(sink_in, count(c, UNITS, n + 1))
                nc.scalar.activation(sink_term[:, n % 2, :], sink_term[:, n % 2, :],
                                     ACT.Exp).then_inc(exp_done, 1)

            def pt_his(c, n):
                lo, hi = key_tiles(c, n // 2)
                for kt in range(lo, hi):
                    act.wait_ge(pt_done, count(c, 3 * UNITS, 3 * n + kt + 1))
                    act.wait_ge(pv_done, count(c, UNITS, n))
                    nc.scalar.activation(pt_hi[kt], t_bank[kt][:, :], ACT.Copy)\
                      .then_inc(pt_hi_done, signals(lo, hi, kt))

            def take_low(c, n):
                b, kv = divmod(n, 2)
                act.wait_ge(pv_done, count(c, UNITS, n + 1))
                act.wait_ge(at_lo_done, count(c, NB, b))
                nc.scalar.activation(prod[kv * HD:(kv + 1) * HD, :, :],
                                     pv_bank[HD:P, :].rearrange("p (j q) -> p j q", j=G),
                                     ACT.Copy, scale=0.5).then_inc(low_read, 1)

            def normalise(c, n):
                lo, hi = key_tiles(c, n // 2)
                act.wait_ge(den_done, count(c, 2 * UNITS, 2 * n + 2))
                for j in range(2, G):
                    pj = p[:, n % 2, j, lo * P:hi * P]
                    ins = nc.scalar.activation(pj, pj, ACT.Copy, scale=row_sum[:, n % 2, j:j + 1])
                ins.then_inc(norm_act, 1)

            def v_hi_of(c):
                nt = fresh(c) // P
                act.wait_ge(v_turned, count(c, 1, 1))
                act.wait_ge(kvu_moved, count(c, 5, 0))
                ins = nc.scalar.activation(
                    v[:, 2:2 + nt, :, 0, :],
                    t_bank[0][:, 0:nt * P].rearrange("p (b v f) -> p b v f", v=2, f=HD), ACT.Copy)
                if is_first(c):
                    ins = nc.scalar.activation(
                        v[:, 1, :, 0, :], t_bank[1][:, 0:P].rearrange("p (v f) -> p v f", v=2), ACT.Copy)
                ins.then_inc(v_hi_done, 1)

            def merge_hi(c, j):
                act.wait_ge(merged_f, count(c, KD, j + 1))
                nc.scalar.activation(mg_hi[j], gate[:, j % 2, 0, :], ACT.Copy).then_inc(merged_h, 1)

            def attention_hi(c, b):
                act.wait_ge(prod_done, count(c, NB, b + 1))
                nc.scalar.activation(qa[0][:, :, b * P:(b + 1) * P], prod[:, :, :],
                                     ACT.Copy).then_inc(at_hi_done, 1)

            def pooled_his(c, g):
                act.wait_ge(pooled_f, count(c, NG, g + 1))
                act.wait_ge(tile_done, count(c, NW, INDEX[("mix", g - 1)] + 1 if g else 0))
                nc.scalar.activation(pooled_hi, pooled_at(g), ACT.Copy).then_inc(pooled_h, 1)

            def pool_out_hi(c, g):
                act.wait_ge(mix_read, count(c, NG, g + 1))
                nc.scalar.activation(po_hi[:, g, :], zb[:, g % 2, :], ACT.Copy).then_inc(po_hi_done, 1)

            def finish(c, tiles):
                for t in sorted(tiles, key=lambda t: t[0] != "mix"):
                    if t[0] == "mix":
                        pool_out_hi(c, t[1])
                    elif t[0] == "ab":
                        merge_hi(c, t[1])
                    elif t[0] != "out":
                        evacuate(c, t)
                for t in tiles:
                    split(c, INDEX[t] + SPLITS)

            def square_y(c, blocks):
                for m in blocks:
                    act.wait_ge(y_done, count(c, 8, NB + m + 1))
                    act.wait_ge(y_sq, count(c, NB, m))
                    nc.scalar.activation(junk, y[:, m, :], ACT.Square, scale=D ** -0.5,
                                         accum_out=ssq[:, m:m + 1]).then_inc(y_sq, 1)

            def store(c):
                for m in range(NB):
                    act.wait_ge(y_norm, count(c, NB, m + 1 - NB))
                    act.dma_start(out[bass.ds(c * T - T + m * P, P), :], y[:, m, :])\
                       .then_inc(stored[m], 16)

            def chunk(c):
                for t in HEAD_TILES[:-1]:
                    finish(c, [t])
                    if t == ("k", 0) and not is_first(c):
                        square_y(c - 1, range(2, NB))
                    if t == ("v", 0) and not is_first(c):
                        store(c)
                    if t == ("q", 1):
                        v_hi_of(c)
                for s, tiles in enumerate(STEPS):
                    finish(c, STEPS[s - 1] if s else HEAD_TILES[-1:])
                    if s:
                        pt_his(c, s - 1)
                    if s >= 3 and s % 2 == 1:
                        attention_hi(c, (s - 3) // 2)
                    if s < UNITS:
                        exps(c, s)
                    if s:
                        take_low(c, s - 1)
                    if s < UNITS:
                        normalise(c, s)
                    if s >= 2 and s % 2 == 0:
                        pooled_his(c, s // 2 - 1)
                finish(c, STEPS[-1])
                attention_hi(c, NB - 1)
                finish(c, GATE_TILES[:2])
                for t in GATE_TILES[2:]:
                    finish(c, [t])
                    if t[0] == "ab" and 3 <= t[1] < 3 + NB and not is_last(c):
                        rows_square(c, t[1] - 3)
                w = INDEX[("out", 0)]
                for i in range(8):
                    split(c, w + SPLITS)
                    w += 1
                    if not is_last(c):
                        for k in H_TILES[i]:
                            h_hi_of(c, k)
                square_y(c, range(0, 2))

            over_chunks(act, chunk)
            square_y(LAST, range(2, NB))
            store(CHUNKS)

        @block.vector
        def _(dve):
            def split(c, w):
                if w >= NW and is_last(c):
                    return
                n = cols_of(TILES[w % NW][0])
                dve.wait_ge(split_hi, count(c, NW, w + 1))
                nc.vector.tensor_tensor(w_lo[:, w % SPLITS, 0:n], raw[:, w % RAWS, 0:n],
                                        w_hi[:, w % SPLITS, 0:n].bitcast(F32),
                                        ALU.subtract).then_inc(split_lo, 1)

            def rows_norm(i):
                dve.wait_ge(x_rstd, i + 1)
                nc.vector.scalar_tensor_tensor(xn[:, i, :], xn[:, i, :], rstd[:, 4 + i:5 + i],
                                               g_norm, ALU.mult, ALU.mult).then_inc(x_norm, 1)

            def rows_lo(i, at, b):
                dve.wait_ge(h_hi_done, i)
                for half in range(2):
                    ks = slice(4 * half, 4 * half + 4)
                    ins = nc.vector.tensor_tensor(
                        h_lo[:, ks, at:at + P], bank[b + half][:, :].rearrange("p (k t) -> p k t", k=4),
                        h_hi[:, ks, at:at + P].bitcast(F32), ALU.subtract)
                ins.then_inc(h_lo_done, 1)

            def widen_rstd(c, m):
                dve.wait_ge(x_rstd, count(c, NB, AHEAD + m + 1))
                nc.vector.tensor_scalar(rstd_wide[:, m, :], ident[:, :], 0.0, rstd[:, 4 + m:5 + m],
                                        ALU.mult, ALU.add).then_inc(rstd_made, 1)

            def scale_x_t(c, k):
                dve.wait_ge(xt_in[k % XTS], count(c, KD // XTS, k // XTS + 1, 16))
                if k == 0:
                    dve.wait_ge(rstd_turned, count(c, 1, 1))
                nc.vector.scalar_tensor_tensor(xt[:, k % XTS, :], rstd_bank[:, :], g_col[:, k:k + 1],
                                               xt[:, k % XTS, :], ALU.mult, ALU.mult).then_inc(xt_scaled, 1)

            def h_lo_of(c, k):
                dve.wait_ge(h_hi_done, count(c, KD, AHEAD + k + 1))
                nc.vector.tensor_tensor(h_lo[:, k, P:P + T], xt[:, k % XTS, :],
                                        h_hi[:, k, P:P + T].bitcast(F32), ALU.subtract)\
                  .then_inc(h_lo_done, 1)

            dve.wait_ge(gain_in, 16)
            for i in range(AHEAD + 2):
                if i < AHEAD:
                    rows_norm(i)
                if i >= 2:
                    rows_lo(i - 1, (i - 2) * P, 2 + 2 * ((i - 2) % 3))
                if i == 2:
                    split(0, 0)
            for w in range(1, SPLITS):
                split(0, w)
            dve.wait_ge(s_const, 16 * N_CONST)
            dve.wait_ge(s_abs, 1)
            dist = arena_f[:, 5 * D:5 * D + 3 * P]
            for hd in range(NH):
                nc.vector.tensor_scalar(bias[:, hd, :], dist, -(2.0 ** -(hd + 1)), None,
                                        ALU.mult).then_inc(s_cdve, 1)
            nc.vector.tensor_scalar(minus_sink[:, :], sink[:, :], -1.0, None, ALU.mult).then_inc(s_cdve, 1)
            nc.vector.tensor_scalar(half_scale[:, :], half_scale[:, :], 0.5, None,
                                    ALU.mult).then_inc(s_cdve, 1)
            dve.wait_ge(s_made, 8)
            nc.vector.reciprocal(recip[:, :], recip[:, :]).then_inc(s_cdve, 1)
            nc.vector.reciprocal(recip_down[:, :], recip_down[:, :]).then_inc(s_cdve, 1)
            dve.wait_ge(s_cdve, 8 + 4)
            dve.wait_ge(s_made, 10)

            def evacuate(c, t):
                kind, j = t
                src = dense_bank(t)
                n = fresh(c)
                if kind == "k":
                    dve.wait_ge(hi_kq, count(c, 5, 1))
                    for kv in range(2):
                        rows = slice(kv * HD, (kv + 1) * HD)
                        ins = nc.vector.tensor_tensor(
                            k_lo[rows, 2 * P:2 * P + n], src[rows, 0:n],
                            k_hi[kv][rows, 2 * P:2 * P + n].bitcast(F32), ALU.subtract)
                        if is_first(c):
                            ins = nc.vector.tensor_tensor(
                                k_lo[rows, P:2 * P], bank[0][rows, 0:P],
                                k_hi[kv][rows, P:2 * P].bitcast(F32), ALU.subtract)
                    ins.then_inc(dve_read, 1)
                elif kind == "q":
                    dve.wait_ge(hi_kq, count(c, 5, j + 2))
                    for kv in range(2):
                        rows, to = slice(kv * HD, (kv + 1) * HD), slice((1 - kv) * HD, (2 - kv) * HD)
                        ins = nc.vector.scalar_tensor_tensor(
                            qa[kv][to, j, :], src[rows, :], HD ** -0.5, qa[kv][rows, j, :].bitcast(F32),
                            ALU.mult, ALU.subtract)
                    ins.then_inc(dve_read, 1)
                elif kind in ("za", "zb"):
                    dst = za[:, j, :] if kind == "za" else zb[:, j % 2, :]
                    dve.wait_ge(tanh_z, count(c, 8, (0 if kind == "za" else 4) + j + 1))
                    nc.vector.scalar_tensor_tensor(dst, dst, 1.0, src[:, :], ALU.add,
                                                   ALU.mult).then_inc(dve_read, 1)

            def maxima(c, n):
                b, kv = divmod(n, 2)
                lo, hi = key_tiles(c, b)
                for j in range(G):
                    dve.wait_ge(qk_done, count(c, 4 * UNITS, 4 * n + j + 1))
                    if j == 0:
                        dve.wait_ge(pt_done, count(c, 3 * UNITS, 3 * (n - 1)))
                    nc.vector.memset(waiter[:, n % 2, j:j + 1], 0.0)
                    nc.vector.tensor_tensor_reduce(
                        p[:, n % 2, j, lo * P:hi * P], bank[j % 2][:, lo * P:hi * P],
                        bias[:, kv * G + j, lo * P:hi * P], 1.0, -3.0e38, ALU.add, ALU.max,
                        row_max[:, n % 2, j:j + 1]).then_inc(max_done, 1)
                dve.wait_ge(max_done, count(c, 4 * UNITS, 4 * n + 4))
                nc.vector.scalar_tensor_tensor(minus_max[:, n % 2, :], row_max[:, n % 2, :], -1.0,
                                               minus_sink[:, kv * G:kv * G + G], ALU.mult,
                                               ALU.min).then_inc(neg_done, 1)
                dve.wait_ge(neg_done, count(c, UNITS, n + 1))
                nc.vector.tensor_tensor(sink_term[:, n % 2, :], sink[:, kv * G:kv * G + G],
                                        minus_max[:, n % 2, :], ALU.add).then_inc(sink_in, 1)

            def normalise(c, n):
                lo, hi = key_tiles(c, n // 2)
                dve.wait_ge(exp_done, count(c, UNITS, n + 1))
                nc.vector.tensor_tensor(row_sum[:, n % 2, :], row_sum[:, n % 2, :],
                                        sink_term[:, n % 2, :], ALU.add).then_inc(den_done, 1)
                dve.wait_ge(den_done, count(c, 2 * UNITS, 2 * n + 1))
                nc.vector.reciprocal(row_sum[:, n % 2, :], row_sum[:, n % 2, :]).then_inc(den_done, 1)
                dve.wait_ge(den_done, count(c, 2 * UNITS, 2 * n + 2))
                for j in range(2):
                    pj = p[:, n % 2, j, lo * P:hi * P]
                    ins = nc.vector.tensor_scalar(pj, pj, row_sum[:, n % 2, j:j + 1], None, ALU.mult)
                ins.then_inc(norm_done, 1)

            def pt_los(c, n):
                lo, hi = key_tiles(c, n // 2)
                for kt in range(lo, hi):
                    dve.wait_ge(pt_hi_done, count(c, 3 * UNITS, 3 * n + kt + 1))
                    nc.vector.tensor_tensor(pt_lo[kt], t_bank[kt][:, :], pt_hi[kt].bitcast(F32),
                                            ALU.subtract).then_inc(pt_lo_done, signals(lo, hi, kt))

            def output_sum(c, n):
                rows = slice(n % 2 * HD, (n % 2 + 1) * HD)
                dve.wait_ge(low_read, count(c, UNITS, n + 1))
                nc.vector.scalar_tensor_tensor(prod[rows, :, :],
                                               pv_bank[0:HD, :].rearrange("p (j q) -> p j q", j=G), 0.5,
                                               prod[rows, :, :], ALU.mult, ALU.add).then_inc(pv_read, 1)

            def pooled(c, g):
                win = WINDOWS[g]
                total = sums[:, g % 2, :]
                here = u[:, g, LEFT:LEFT + T]
                dve.wait_ge(sum_step, count(c, 10, (g + 1) * (g + 2) // 2))
                lo = win // 2 if is_first(c) else 0
                hi = T - (win // 2 - 1) if is_last(c) else T
                ends = []
                if lo:
                    ends.append((slice(0, lo), recip[:, win // 2 - 1:win - 1]))
                if hi < T:
                    ends.append((slice(hi, T), recip_down[:, 16 - win + 1:16 - win // 2]))
                for cols, r in ends:
                    nc.vector.tensor_tensor(total[:, cols], total[:, cols], r, ALU.mult)\
                      .then_inc(edge_done, 1)
                    edges[0] += 1
                    dve.wait_ge(edge_done, edges[0])
                    nc.vector.tensor_tensor(pooled_at(g)[:, cols], total[:, cols], here[:, cols],
                                            ALU.subtract)
                nc.vector.scalar_tensor_tensor(pooled_at(g)[:, lo:hi], total[:, lo:hi], 1.0 / win,
                                               here[:, lo:hi], ALU.mult, ALU.subtract)\
                  .then_inc(pooled_f, 1)

            edges = [0]

            def gate_mixed(c, g):
                dve.wait_ge(tile_done, count(c, NW, INDEX[("mix", g)] + 1))
                nc.vector.scalar_tensor_tensor(zb[:, g % 2, :], mix_bank[:, :],
                                               half_scale[:, g:g + 1], zb[:, g % 2, :], ALU.mult,
                                               ALU.mult).then_inc(mix_read, 1)

            def merge(c, j):
                dve.wait_ge(tile_done, count(c, NW, INDEX[("ab", j)] + 1))
                dve.wait_ge(*last_read(c, ("gb", j)))
                for a in range(2):
                    gt = gate[:, j % 2, a, :]
                    nc.vector.scalar_tensor_tensor(gt, gt, 1.0, bank[2 * (j % 2) + a][:, :], ALU.add,
                                                   ALU.mult).then_inc(gated, 1)
                dve.wait_ge(gated, count(c, 2 * KD, 2 * j + 2))
                nc.vector.tensor_tensor(gate[:, j % 2, 0, :], gate[:, j % 2, 0, :], gate[:, j % 2, 1, :],
                                        ALU.add).then_inc(merged_f, 1)
                dve.wait_ge(merged_h, count(c, KD, j + 1))
                nc.vector.tensor_tensor(mg_lo[j], gate[:, j % 2, 0, :], mg_hi[j].bitcast(F32),
                                        ALU.subtract).then_inc(merged_l, 1)

            def carry_kvu(c):
                dve.wait_ge(pv_done, count(c, UNITS, UNITS))
                dve.wait_ge(sum_step, count(c, 10, 10))
                for t in (*k_hi, k_lo):
                    nc.vector.tensor_copy(t[:, 0:2 * P], t[:, T:T + 2 * P].bitcast(F32))\
                      .then_inc(kvu_moved, 1)
                nc.vector.tensor_copy(v[:, 0:2, :, :, :], v[:, NB:NB + 2, :, :, :].bitcast(F32))\
                  .then_inc(kvu_moved, 1)
                nc.vector.tensor_copy(u[:, :, 0:FRESH], u[:, :, T:T + FRESH]).then_inc(kvu_moved, 1)

            def v_lo_of(c):
                nt = fresh(c) // P
                dve.wait_ge(v_hi_done, count(c, 1, 1))
                ins = nc.vector.tensor_tensor(
                    v[:, 2:2 + nt, :, 1, :],
                    t_bank[0][:, 0:nt * P].rearrange("p (b v f) -> p b v f", v=2, f=HD),
                    v[:, 2:2 + nt, :, 0, :].bitcast(F32), ALU.subtract)
                if is_first(c):
                    ins = nc.vector.tensor_tensor(
                        v[:, 1, :, 1, :], t_bank[1][:, 0:P].rearrange("p (v f) -> p v f", v=2),
                        v[:, 1, :, 0, :].bitcast(F32), ALU.subtract)
                ins.then_inc(v_lo_done, 1)

            def add_residual(c, side):
                half = slice(side * T, (side + 1) * T)
                for m in range(NB):
                    if m < NB - 1:
                        dve.wait_ge(out_done, count(c, 2 * (NB - 1), side * (NB - 1) + m + 1))
                    else:
                        dve.wait_ge(tile_done, count(c, NW, INDEX[("out", 4 * side + 3)] + 1))
                    dve.wait_ge(res_in[m], count(c, 1, 1, 16))
                    nc.vector.scalar_tensor_tensor(y[:, m, half], bank[m][:, :], 0.5, y[:, m, half],
                                                   ALU.mult, ALU.add).then_inc(y_done, 1)

            def normalise_y(c, blocks):
                for m in blocks:
                    dve.wait_ge(y_rstd, count(c, NB, m + 1))
                    nc.vector.scalar_tensor_tensor(y[:, m, :], y[:, m, :], rstd[:, m:m + 1],
                                                   g_final[:, :], ALU.mult, ALU.mult).then_inc(y_norm, 1)

            def finish(c, tiles):
                for t in tiles:
                    if t[0] == "ab":
                        merge(c, t[1])
                    elif t[0] not in ("mix", "out"):
                        evacuate(c, t)
                for t in tiles:
                    split(c, INDEX[t] + SPLITS)

            def chunk(c):
                for t in HEAD_TILES[:-1]:
                    finish(c, [t])
                    if t == ("k", 0) and not is_first(c):
                        normalise_y(c - 1, range(2, NB))
                    if t == ("q", 1):
                        v_lo_of(c)
                for s, tiles in enumerate(STEPS):
                    if s == UNITS:
                        finish(c, STEPS[s - 1])
                    if s < UNITS:
                        maxima(c, s)
                    if s:
                        pt_los(c, s - 1)
                    if s < UNITS:
                        finish(c, STEPS[s - 1] if s else HEAD_TILES[-1:])
                    if tiles[0][0] == "mix":
                        gate_mixed(c, tiles[0][1])
                    if s < UNITS:
                        normalise(c, s)
                    if s == UNITS:
                        output_sum(c, s - 1)
                    if s >= 2 and s % 2 == 0:
                        pooled(c, s // 2 - 1)
                    if 0 < s < UNITS:
                        output_sum(c, s - 1)
                finish(c, STEPS[-1])
                gate_mixed(c, NG - 1)
                finish(c, GATE_TILES[:2])
                for t in GATE_TILES[2:]:
                    finish(c, [t])
                    if t == ("ab", 2) and not is_last(c):
                        carry_kvu(c)
                if not is_last(c):
                    for m in range(NB):
                        widen_rstd(c, m)
                for i in range(8):
                    if i == 0 and not is_last(c):
                        dve.wait_ge(tile_done, count(c, NW, INDEX[("ab", KD - 1)] + 1))
                        for t in (h_hi, h_lo):
                            nc.vector.tensor_copy(t[:, :, 0:P], t[:, :, T:T + P].bitcast(F32))\
                              .then_inc(h_moved, 1)
                    if i == 3:
                        add_residual(c, 0)
                    if not is_last(c):
                        for k in H_TILES[i]:
                            scale_x_t(c, k)
                    split(c, INDEX[("out", i)] + SPLITS)
                    if not is_last(c):
                        for k in H_TILES[i]:
                            h_lo_of(c, k)
                add_residual(c, 1)
                normalise_y(c, range(0, 2))

            over_chunks(dve, chunk)
            normalise_y(LAST, range(2, NB))

        @block.tensor
        def _(pe):
            def passes(dst, a, b, start, stop):
                nc.tensor.matmul(dst, a[0], b[0], start=start, stop=False)
                nc.tensor.matmul(dst, a[0], b[1], start=False, stop=False)
                return nc.tensor.matmul(dst, a[1], b[0], start=False, stop=stop)

            def w_at(w, k):
                cols = slice(k * P, (k + 1) * P)
                return w_hi[:, w % SPLITS, cols], w_lo[:, w % SPLITS, cols]

            def h_at(k, lo, n):
                return h_hi[:, k, lo:lo + n], h_lo[:, k, lo:lo + n]

            def turn_rows(i, b):
                pe.wait_ge(x_norm, i + 1)
                if i >= 3:
                    pe.wait_ge(h_lo_done, i - 2)
                for k in range(KD):
                    ins = nc.tensor.transpose(bank[b + k // 4][:, (k % 4) * P:(k % 4 + 1) * P],
                                              xn[:, i, k * P:(k + 1) * P], ident[:, :])
                ins.then_inc(x_turned, 1)

            def turn_rstd(c):
                for m in range(NB):
                    pe.wait_ge(rstd_made, count(c, NB, m + 1))
                    ins = nc.tensor.transpose(rstd_bank[:, m * P:(m + 1) * P], rstd_wide[:, m, :],
                                              ident[:, :])
                ins.then_inc(rstd_turned, 1)

            def dense(c, t, ks=range(KD)):
                kind, j = t
                w = INDEX[t]
                ahead = kind in ("k", "v", "u")
                n = fresh(c) if ahead else T
                at = P if ahead else 0
                dst = dense_bank(t)
                if ks[0] == 0:
                    i = DENSE.index(t)
                    pe.wait_ge(split_lo, count(c, NW, w + 1))
                    pe.wait_ge(*last_read(c, DENSE[i - 2], back=1 if i < 2 else 0))
                for k in ks:
                    ins = passes(dst[:, 0:n], w_at(w, k), h_at(k, at, n), k == 0, k == KD - 1)
                if ks[-1] == KD - 1:
                    if is_first(c) and kind in ("v", "u"):
                        dst = bank[1] if kind == "v" else u_bank
                        if kind == "u":
                            pe.wait_ge(pt_lo_done, count(c, 3 * UNITS, 6 * j))
                        for k in range(KD):
                            ins = passes(dst[:, 0:P], w_at(w, k), h_at(k, 0, P), k == 0, k == KD - 1)
                    ins.then_inc(tile_done, 1)

            def turn_v(c):
                pe.wait_ge(*last_read(c, ("v", 0)))
                pe.wait_ge(y_done, count(c, 8, 0))
                for b in range(fresh(c) // P):
                    ins = nc.tensor.transpose(t_bank[0][:, b * P:(b + 1) * P], v_t[:, b * P:(b + 1) * P],
                                              ident[:, :])
                if is_first(c):
                    ins = nc.tensor.transpose(t_bank[1][:, 0:P], v_t[:, T:T + P], ident[:, :])
                ins.then_inc(v_turned, 1)

            def scores(c, n, heads):
                b, kv = divmod(n, 2)
                lo, hi = key_tiles(c, b)
                rows = slice(kv * HD, (kv + 1) * HD)
                keys = slice((b + lo) * P, (b + hi) * P)
                if n == 0:
                    pe.wait_ge(*last_read(c, ("q", 3)))
                for j in heads:
                    if j == 1 and n >= 4 and n % 2 == 0:
                        pe.wait_ge(mix_read, count(c, NG, (n - 2) // 2))
                    pe.wait_ge(max_done, count(c, 4 * UNITS, 4 * n + j - 1))
                    queries = slice(b * P, (b + 1) * P)
                    dst = bank[j % 2][:, lo * P:hi * P]
                    nc.tensor.matmul(dst, qa[kv][:, j, queries], k_hi[kv][:, keys], start=True,
                                     stop=False)
                    nc.tensor.matmul(dst, qa[kv][rows, j, queries], k_lo[rows, keys], start=False,
                                     stop=True).then_inc(qk_done, 1)

            def turn_p(c, n):
                lo, hi = key_tiles(c, n // 2)
                pe.wait_ge(norm_done, count(c, UNITS, n + 1))
                pe.wait_ge(norm_act, count(c, UNITS, n + 1))
                for kt in range(lo, hi):
                    pe.wait_ge(pt_lo_done, count(c, 3 * UNITS, 3 * (n - 1) + kt + 1))
                    if is_first(c) and kt == 2:
                        pe.wait_ge(*last_read(c, ("u", n // 2)))
                    for j in range(G):
                        ins = nc.tensor.transpose(t_bank[kt][:, j * P:(j + 1) * P],
                                                  p[:, n % 2, j, kt * P:(kt + 1) * P], ident[:, :])
                    ins.then_inc(pt_done, signals(lo, hi, kt))

            def values(c, n):
                b, kv = divmod(n, 2)
                lo, hi = key_tiles(c, b)
                pe.wait_ge(pv_read, count(c, UNITS, n))
                if n == 0:
                    pe.wait_ge(v_lo_done, count(c, 1, 1))
                for kt in range(lo, hi):
                    pe.wait_ge(pt_lo_done, count(c, 3 * UNITS, 3 * n + kt + 1))
                    v_block = v[:, b + kt, kv, :, :]
                    nc.tensor.matmul(pv_bank[:, :], v_block, pt_hi[kt], start=kt == lo, stop=False)
                    ins = nc.tensor.matmul(pv_bank[:, :], v_block, pt_lo[kt], start=False,
                                           stop=kt == hi - 1)
                ins.then_inc(pv_done, 1)

            def mix(c, g):
                w = INDEX[("mix", g)]
                pe.wait_ge(split_lo, count(c, NW, w + 1))
                pe.wait_ge(max_done, count(c, 4 * UNITS, 4 * min(2 * g + 4, UNITS)))
                pe.wait_ge(pooled_l, count(c, NG, g + 1))
                passes(mix_bank[:, :], w_at(w, 0), (pooled_hi, pooled_lo), True,
                       True).then_inc(tile_done, 1)

            def branches(c, j):
                w = INDEX[("ab", j)]
                pe.wait_ge(split_lo, count(c, NW, w + 1))
                if j:
                    pe.wait_ge(gated, count(c, 2 * KD, 2 * (j - 1)))
                for a, (hi, lo) in enumerate((qa, (po_hi, po_lo))):
                    if j == 0 and a == 0:
                        pe.wait_ge(at_lo_done, count(c, NB, NB))
                    if j == 0 and a == 1:
                        pe.wait_ge(po_lo_done, count(c, NG, NG))
                    for k in range(4):
                        ins = passes(bank[2 * (j % 2) + a][:, :], w_at(w, 4 * a + k),
                                     (hi[:, k, :], lo[:, k, :]), k == 0, k == 3)
                ins.then_inc(tile_done, 1)

            def output(c, i):
                w = INDEX[("out", i)]
                half, pair = divmod(i, 4)
                pe.wait_ge(split_lo, count(c, NW, w + 1))
                if half == 0:
                    pe.wait_ge(merged_l, count(c, KD, 2 * pair + 2))
                for m in range(NB):
                    if i == 0 and m == 2:
                        pe.wait_ge(gated, count(c, 2 * KD, 2 * KD))
                    if pair == 0 and half == 1:
                        pe.wait_ge(y_done, count(c, 8, m + 1))
                    for e in range(2):
                        k = 2 * pair + e
                        tok = slice(m * P, (m + 1) * P)
                        rhs = (w_hi[:, w % SPLITS, e * T:(e + 1) * T],
                               w_lo[:, w % SPLITS, e * T:(e + 1) * T])
                        ins = passes(bank[m][:, :], (mg_hi[k][:, tok], mg_lo[k][:, tok]), rhs,
                                     k == 0, k == KD - 1)
                    if pair == 3 and m < NB - 1:
                        ins.then_inc(out_done, 1)
                ins.then_inc(tile_done, 1)

            pe.wait_ge(s_made, 5)
            for i in range(AHEAD):
                turn_rows(i, 2 + 2 * (i % 3))
                if i == 2:
                    pe.wait_ge(h_lo_done, 1)
                    pe.wait_ge(split_lo, 1)
                for k in {2: range(4), 3: range(4, KD)}.get(i, ()):
                    passes(bank[0][:, 0:P], w_at(0, k), h_at(k, 0, P), k == 0, k == KD - 1)

            def chunk(c):
                if is_first(c):
                    pe.wait_ge(h_lo_done, AHEAD)
                else:
                    pe.wait_ge(h_lo_done, count(c, KD, AHEAD))
                for t in HEAD_TILES:
                    dense(c, t)
                    if t == ("q", 1):
                        turn_v(c)
                for s, tiles in enumerate(STEPS):
                    before = 2 if s < UNITS else 4
                    after = 7 if s < UNITS else KD
                    if s < UNITS:
                        scores(c, s, range(0, 2))
                    dense(c, tiles[-1], range(0, before))
                    if s < UNITS:
                        scores(c, s, range(2, G))
                    if s:
                        turn_p(c, s - 1)
                    dense(c, tiles[-1], range(before, after))
                    if len(tiles) > 1:
                        mix(c, tiles[0][1])
                    if s:
                        values(c, s - 1)
                    if after < KD:
                        dense(c, tiles[-1], range(after, KD))
                for t in GATE_TILES:
                    if t[0] == "ab":
                        branches(c, t[1])
                    elif t[0] == "mix":
                        mix(c, t[1])
                    else:
                        dense(c, t)
                for i in range(8):
                    output(c, i)
                    if i == 1 and not is_last(c):
                        turn_rstd(c)

            over_chunks(pe, chunk)


def kernel(x, norm_g, w_in, attn_sink, pool_w, pool_scale, w_branch_a, w_branch_b, w_out, final_norm_g):
    import numpy as np
    import concourse.bacc as bacc
    from concourse.bass_utils import run_bass_kernel_spmd

    def lay(a):
        return np.ascontiguousarray(a)

    heads = np.arange(NH * HD).reshape(2, G, HD).transpose(1, 0, 2).ravel()
    w = np.asarray(w_in)[0]
    off = np.cumsum([0, 512, 128, 128, 512, 512, 512, 1024, 1024])
    cols = np.concatenate([heads, np.arange(off[1], off[3]), off[3] + heads, np.arange(off[4], off[8])])
    w_in_t = lay(w[:, cols].reshape(KD, P, -1, P).transpose(2, 1, 0, 3).reshape(-1, P, D))
    ab = np.concatenate([np.asarray(w_branch_a)[0][heads], np.asarray(w_branch_b)[0]])
    w_ab_t = lay(ab.reshape(8, P, KD, P).transpose(2, 1, 0, 3).reshape(KD, P, D))
    w_out_t = lay(np.asarray(w_out)[0].reshape(4, 2, P, 2, T).transpose(3, 0, 2, 1, 4).reshape(8, P, D))
    rows = np.asarray(x)[0]
    x_t = lay(np.concatenate([rows, rows[:P]]).T.reshape(KD, P, S + P))
    arrays = {
        "in_x": lay(rows), "in_x_t": x_t, "in_w_in": w_in_t, "in_w_ab": w_ab_t, "in_w_out": w_out_t,
        "in_pool_w": lay(np.asarray(pool_w)[0]), "in_sink": lay(np.asarray(attn_sink)),
        "in_pool_scale": lay(np.asarray(pool_scale).reshape(NG, P)), "in_norm_g": lay(np.asarray(norm_g)),
        "in_norm_g_t": lay(np.asarray(norm_g).reshape(KD, P).T),
        "in_final_g": lay(np.asarray(final_norm_g).reshape(1, D)),
    }
    nc = bacc.Bacc("TRN2", target_bir_lowering=False, num_devices=1)
    ap = {k: nc.dram_tensor(k, a.shape, mybir.dt.from_np(a.dtype), kind="ExternalInput").ap()
          for k, a in arrays.items()}
    out = nc.dram_tensor("out", (S, D), F32, kind="ExternalOutput").ap()
    build(nc, ap["in_x"], ap["in_x_t"], ap["in_w_in"], ap["in_w_ab"], ap["in_w_out"],
          ap["in_pool_w"], ap["in_sink"], ap["in_pool_scale"], ap["in_norm_g"], ap["in_norm_g_t"],
          ap["in_final_g"], out)
    r = run_bass_kernel_spmd(nc, [arrays], core_ids=[0])
    return r.results[0]["out"].reshape(1, S, D)
```
